# Optimizing a Trainium2 kernel written in Bass

```python
import math
import jax, jax.numpy as jnp
from jax import lax
import numpy as np

D_MODEL = 2048
BATCH = 1
SEQ = 256
DEPTH = 2
DEC_BATCH = 8
DEC_SEQ = 1
PAST_LEN = 256
PAGE_SIZE = 128

HS = 64
D_A = D_MODEL // 2
H_A = D_A // HS
R_W = 64
R_A = 64
R_V = 32
GN_EPS = 64e-5
HD = 64
D_B = D_MODEL // 2
H_B = D_B // HD
G_KV = 4
R_Q = H_B // G_KV
KV_W = G_KV * HD
CMP_LEN = 32
CMP_STRIDE = 16
CMP_HID = 128
SEL_LEN = 64
N_TOP = 16
WIN = 512
Q_BLOCK = 32
NUM_BUCKETS = 32
MAX_DIST = 128
SCALE = HD ** -0.5
A_COLS = 4 * D_A + R_W + R_A
B_COLS = 2 * D_B + 6 * KV_W + 3 * H_B
IN_COLS = A_COLS + B_COLS + 2 * D_MODEL
ALPHA = (2 * DEPTH) ** 0.25
BETA = (8 * DEPTH) ** -0.25
LN_EPS = 1e-5
NEG = -1e30

kernel_name = 'hybrid_rwkv7_nsa_decoder_step'

def split_cols(x, sizes):
    return jnp.split(x, np.cumsum(sizes)[:-1].tolist(), axis=-1)

def layer_norm(x, g, b):
    xf = x.astype(jnp.float32)
    mu = xf.mean(-1, keepdims=True)
    var = jnp.square(xf - mu).mean(-1, keepdims=True)
    return ((xf - mu) * lax.rsqrt(var + LN_EPS) * g + b).astype(x.dtype)

def masked_softmax(s, mask):
    s = jnp.where(mask, s.astype(jnp.float32), NEG)
    return jnp.where(mask, jax.nn.softmax(s, axis=-1), 0.0)

def t5_bucket(dist):
    n = jnp.maximum(dist, 0)
    max_exact = NUM_BUCKETS // 2
    nf = jnp.maximum(n, 1).astype(jnp.float32)
    large = max_exact + (jnp.log(nf / max_exact) / math.log(MAX_DIST / max_exact)
                         * (NUM_BUCKETS - max_exact)).astype(jnp.int32)
    large = jnp.minimum(large, NUM_BUCKETS - 1)
    return jnp.where(n < max_exact, n, large)

def t5_bias(table, dist):
    b = t5_bucket(dist)
    tg = table.reshape(NUM_BUCKETS, G_KV, R_Q)
    out = tg[b, jnp.arange(G_KV)[:, None]]
    return jnp.swapaxes(out, -1, -2).astype(jnp.float32)

def rwkv_scan(r, w, k, v, a, b, s0):
    def step(S, inp):
        r_t, w_t, k_t, v_t, a_t, b_t = inp
        sa = jnp.einsum('bhij,bhj->bhi', S, a_t)
        S = S * w_t[:, :, None, :] + sa[..., None] * b_t[:, :, None, :] + v_t[..., None] * k_t[:, :, None, :]
        return S, jnp.einsum('bhij,bhj->bhi', S, r_t)
    xs = (r, w, k, v, a, b)
    xs = tuple(jnp.moveaxis(u, 1, 0) for u in xs)
    s_fin, ys = lax.scan(step, s0, xs)
    return jnp.moveaxis(ys, 0, 1), s_fin

def rwkv_mixer(fa, s0, v_first, l, p):
    bsz, t = fa.shape[:2]
    r, k, v, w_lo, a_lo, z = split_cols(fa, [D_A, D_A, D_A, R_W, R_A, D_A])
    w_log = -jax.nn.softplus(-(p['rw_w0'][l] + jnp.tanh(w_lo) @ p['rw_w2'][l])) - 0.5
    decay = jnp.exp(-jnp.exp(w_log.astype(jnp.float32)))
    if l == 0:
        v_first = v
    else:
        vg = jax.nn.sigmoid(p['rw_v0'][l - 1] + (v @ p['rw_v1'][l - 1]) @ p['rw_v2'][l - 1])
        v = v + (v_first - v) * vg
    a = jax.nn.sigmoid(p['rw_a0'][l] + a_lo @ p['rw_a2'][l])
    heads = lambda u: u.reshape(bsz, t, H_A, HS).astype(jnp.float32)
    kk = heads(k * p['rw_kk'][l])
    kk = kk * lax.rsqrt(jnp.maximum(jnp.sum(kk * kk, -1, keepdims=True), 1e-24))
    k = k * (1.0 + (a - 1.0) * p['rw_ka'][l])
    rh, kh, vh, ah = heads(r), heads(k), heads(v), heads(a)
    y, s_fin = rwkv_scan(rh, heads(decay), kh, vh, -kk, kk * ah, s0)
    mu = y.mean(-1, keepdims=True)
    var = jnp.square(y - mu).mean(-1, keepdims=True)
    yn = ((y - mu) * lax.rsqrt(var + GN_EPS)).reshape(bsz, t, D_A) * p['rw_gn_g'][l] + p['rw_gn_b'][l]
    bonus = (jnp.sum(rh * kh * p['rw_rk'][l], -1, keepdims=True) * vh).reshape(bsz, t, D_A)
    o = (yn + bonus) * jax.nn.silu(z.astype(jnp.float32))
    return o.astype(fa.dtype), s_fin, v_first

def compress(rows, w1, b1, w2, b2):
    bsz, t = rows.shape[:2]
    nch = t // CMP_STRIDE
    ch = rows[:, :nch * CMP_STRIDE].reshape(bsz, nch, CMP_STRIDE, G_KV, HD)
    ch = ch.transpose(0, 1, 3, 2, 4).reshape(bsz, nch, G_KV, CMP_STRIDE * HD)
    half = CMP_STRIDE * HD
    h = ch[:, :-1] @ w1[:half] + ch[:, 1:] @ w1[half:] + b1
    return jax.nn.gelu(h) @ w2 + b2

def to_blocks(rows):
    bsz, t = rows.shape[:2]
    nsel = -(-t // SEL_LEN)
    rows = jnp.pad(rows, ((0, 0), (0, nsel * SEL_LEN - t), (0, 0), (0, 0)))
    return rows.reshape(bsz, nsel, SEL_LEN, G_KV, HD)

def nsa_attend(q, q_pos, k_cmp, v_cmp, ks_blk, vs_blk, kw, vw, kw_pos, gates, table):
    bsz, tq = q.shape[:2]
    nc, nsel = k_cmp.shape[1], ks_blk.shape[1]
    cmp_end = jnp.arange(nc, dtype=jnp.int32) * CMP_STRIDE + CMP_LEN - 1
    dist_c = q_pos[:, None] - cmp_end[None, :]
    s_c = jnp.einsum('btgrd,bngd->btgrn', q, k_cmp) * SCALE
    s_c = s_c + t5_bias(table, jnp.broadcast_to(dist_c[:, None, :], (tq, G_KV, nc)))[None]
    p_c = masked_softmax(s_c, (dist_c >= 0)[None, :, None, None, :])
    o_c = jnp.einsum('btgrn,bngd->btgrd', p_c, v_cmp)
    ci = jnp.arange(nc)[:, None] * CMP_STRIDE
    sj = jnp.arange(nsel)[None, :] * SEL_LEN
    overlap = ((ci < sj + SEL_LEN) & (ci + CMP_LEN > sj)).astype(jnp.float32)
    imp = jnp.einsum('btgrn,ns->btgs', p_c, overlap)
    blk = jnp.arange(nsel, dtype=jnp.int32)[None, :]
    cur = (q_pos // SEL_LEN)[:, None]
    valid = blk * SEL_LEN <= q_pos[:, None]
    forced = (blk == 0) | (blk == cur) | (blk == cur - 1)
    imp = jnp.where(valid[None, :, None, :], imp, NEG)
    imp = jnp.where(forced[None, :, None, :], -NEG, imp)
    top_v, top_i = lax.top_k(imp, min(N_TOP, nsel))
    n_sel = top_i.shape[-1]
    top_ok = top_v > 0.5 * NEG
    kb = ks_blk.transpose(0, 3, 1, 2, 4).reshape(bsz, G_KV, nsel, SEL_LEN * HD)
    vb = vs_blk.transpose(0, 3, 1, 2, 4).reshape(bsz, G_KV, nsel, SEL_LEN * HD)
    idx = top_i.transpose(0, 2, 1, 3).reshape(bsz, G_KV, tq * n_sel)[..., None]
    gather = lambda src: jnp.take_along_axis(src, idx, axis=2).reshape(
        bsz, G_KV, tq, n_sel * SEL_LEN, HD).transpose(0, 2, 1, 3, 4)
    k_sel, v_sel = gather(kb), gather(vb)
    pos_sel = (top_i[..., None] * SEL_LEN + jnp.arange(SEL_LEN, dtype=jnp.int32)).reshape(bsz, tq, G_KV, n_sel * SEL_LEN)
    dist_s = q_pos[None, :, None, None] - pos_sel
    mask_s = (dist_s >= 0) & jnp.repeat(top_ok, SEL_LEN, axis=-1)
    s_s = jnp.einsum('btgrd,btgkd->btgrk', q, k_sel) * SCALE + t5_bias(table, dist_s)
    p_s = masked_softmax(s_s, mask_s[..., None, :])
    o_s = jnp.einsum('btgrk,btgkd->btgrd', p_s, v_sel)
    dist_w = q_pos[:, None] - kw_pos[None, :]
    mask_w = (dist_w >= 0) & (dist_w < WIN) & (kw_pos[None, :] >= 0)
    s_w = jnp.einsum('btgrd,bkgd->btgrk', q, kw) * SCALE
    s_w = s_w + t5_bias(table, jnp.broadcast_to(dist_w[:, None, :], (tq, G_KV, kw.shape[1])))[None]
    p_w = masked_softmax(s_w, mask_w[None, :, None, None, :])
    o_w = jnp.einsum('btgrk,bkgd->btgrd', p_w, vw)
    return gates[..., 0:1] * o_c + gates[..., 1:2] * o_s + gates[..., 2:3] * o_w

def nsa_prompt(q, kc, vc, ks, vs, kw, vw, gates, cw1, cb1, cw2, cb2, table):
    bsz, t = q.shape[:2]
    k_cmp = compress(kc, cw1[0], cb1[0], cw2[0], cb2[0])
    v_cmp = compress(vc, cw1[1], cb1[1], cw2[1], cb2[1])
    ks_blk, vs_blk = to_blocks(ks), to_blocks(vs)
    pad = ((0, 0), (WIN, 0), (0, 0), (0, 0))
    kw_pad, vw_pad = jnp.pad(kw, pad), jnp.pad(vw, pad)
    nqb = t // Q_BLOCK
    qb = jnp.swapaxes(q.reshape(bsz, nqb, Q_BLOCK, G_KV, R_Q, HD), 0, 1)
    gb = jnp.swapaxes(gates.reshape(bsz, nqb, Q_BLOCK, G_KV, R_Q, 3), 0, 1)
    starts = jnp.arange(nqb, dtype=jnp.int32) * Q_BLOCK

    def one_block(args):
        q_i, g_i, s = args
        kw_i = lax.dynamic_slice_in_dim(kw_pad, s, WIN + Q_BLOCK, axis=1)
        vw_i = lax.dynamic_slice_in_dim(vw_pad, s, WIN + Q_BLOCK, axis=1)
        kw_pos = s - WIN + jnp.arange(WIN + Q_BLOCK, dtype=jnp.int32)
        q_pos = s + jnp.arange(Q_BLOCK, dtype=jnp.int32)
        return nsa_attend(q_i, q_pos, k_cmp, v_cmp, ks_blk, vs_blk, kw_i, vw_i, kw_pos, g_i, table)

    o = lax.map(one_block, (qb, gb, starts))
    return jnp.swapaxes(o, 0, 1).reshape(bsz, t, G_KV, R_Q, HD)

def trunk_layer(x, l, v_first, past, p):
    bsz, t = x.shape[:2]
    h = x @ p['w_in'][l]
    fa, fb, fm = split_cols(h, [A_COLS, B_COLS, 2 * D_MODEL])
    if past is None:
        prev = jnp.pad(fa[:, :-1], ((0, 0), (1, 0), (0, 0)))
        s0 = jnp.zeros((bsz, H_A, HS, HS), jnp.float32)
    else:
        prev = jnp.concatenate([past['shift'][:, None].astype(fa.dtype), fa[:, :-1]], axis=1)
        s0 = past['wkv'].astype(jnp.float32)
    new_shift = fa[:, -1]
    fa_mix = fa + (prev - fa) * p['mu_shift'][l]
    o_a, wkv, v_first = rwkv_mixer(fa_mix, s0, v_first, l, p)
    q, kc, vc, ks, vs, kw, vw, gl, z_b = split_cols(fb, [D_B] + [KV_W] * 6 + [3 * H_B, D_B])
    q = q.reshape(bsz, t, G_KV, R_Q, HD)
    rows = lambda u: u.reshape(bsz, t, G_KV, HD)
    kc, vc, ks, vs, kw, vw = rows(kc), rows(vc), rows(ks), rows(vs), rows(kw), rows(vw)
    gates = jax.nn.sigmoid(gl.reshape(bsz, t, G_KV, R_Q, 3))
    new_rows = jnp.stack([kc, vc, ks, vs], axis=2)
    new_win = jnp.stack([kw, vw], axis=2)
    cw1, cb1, cw2, cb2 = p['cmp_w1'][l], p['cmp_b1'][l], p['cmp_w2'][l], p['cmp_b2'][l]
    if past is None:
        o_b = nsa_prompt(q, kc, vc, ks, vs, kw, vw, gates, cw1, cb1, cw2, cb2, p['rel_bias'])
        win_state = new_win[:, -min(WIN, t):]
    else:
        past_len = past['kv'].shape[1]
        all_rows = jnp.concatenate([past['kv'].astype(new_rows.dtype), new_rows], axis=1)
        k_cmp = compress(all_rows[:, :, 0], cw1[0], cb1[0], cw2[0], cb2[0])
        v_cmp = compress(all_rows[:, :, 1], cw1[1], cb1[1], cw2[1], cb2[1])
        ks_blk, vs_blk = to_blocks(all_rows[:, :, 2]), to_blocks(all_rows[:, :, 3])
        nbuf = past['win'].shape[1]
        win_all = jnp.concatenate([past['win'].astype(new_win.dtype), new_win], axis=1)
        kw_pos = past_len - nbuf + jnp.arange(nbuf + t, dtype=jnp.int32)
        q_pos = past_len + jnp.arange(t, dtype=jnp.int32)
        o_b = nsa_attend(q, q_pos, k_cmp, v_cmp, ks_blk, vs_blk, win_all[:, :, 0], win_all[:, :, 1],
                         kw_pos, gates, p['rel_bias'])
        win_state = win_all[:, -nbuf:]
    o_b = o_b.reshape(bsz, t, D_B).astype(x.dtype) * jax.nn.silu(z_b)
    g_a, g_b = split_cols(fm, [D_MODEL, D_MODEL])
    merged = jax.nn.sigmoid(g_a) * (o_a @ p['w_up_a'][l]) + jax.nn.sigmoid(g_b) * (o_b @ p['w_up_b'][l])
    y = layer_norm(ALPHA * x + merged @ p['w_out'][l], p['ln_g'][l], p['ln_b'][l])
    return y, v_first, (new_rows, win_state, wkv, new_shift)

def setup_inputs(seed: int = 0) -> dict:
    key = jax.random.key(seed)
    k = jax.random.split(key, 32)
    f32 = jnp.float32
    nrm = lambda kk, shape, s: jax.random.normal(kk, shape, f32) * s
    n_pages = PAST_LEN // PAGE_SIZE
    n_used = DEC_BATCH * n_pages
    n_phys = n_used + max(1, n_used // 4)
    perm = jax.random.permutation(k[6], n_phys)
    page_table = perm[:n_used].reshape(DEC_BATCH, n_pages).astype(jnp.int32)
    return {
        'x_prompt': nrm(k[0], (BATCH, SEQ, D_MODEL), 1.0),
        'x_sample': nrm(k[1], (DEC_BATCH, DEC_SEQ, D_MODEL), 1.0),
        'cache_kv': nrm(k[2], (DEPTH, n_phys, PAGE_SIZE, 4, G_KV, HD), 1.0),
        'cache_win_kv': nrm(k[3], (DEPTH, DEC_BATCH, min(WIN, PAST_LEN), 2, G_KV, HD), 1.0),
        'state_wkv': nrm(k[4], (DEPTH, DEC_BATCH, H_A, HS, HS), 1.0),
        'state_shift': nrm(k[5], (DEPTH, DEC_BATCH, A_COLS), 1.0),
        'page_table': page_table,
        'w_in': nrm(k[7], (DEPTH, D_MODEL, IN_COLS), D_MODEL ** -0.5),
        'mu_shift': jax.random.uniform(k[8], (DEPTH, A_COLS), f32),
        'rw_w0': -1.0 + nrm(k[9], (DEPTH, D_A), 0.5),
        'rw_w2': nrm(k[10], (DEPTH, R_W, D_A), R_W ** -0.5),
        'rw_a0': nrm(k[11], (DEPTH, D_A), 0.1),
        'rw_a2': nrm(k[12], (DEPTH, R_A, D_A), R_A ** -0.5),
        'rw_kk': 0.85 + nrm(k[13], (DEPTH, D_A), 0.05),
        'rw_ka': 1.0 + nrm(k[14], (DEPTH, D_A), 0.05),
        'rw_rk': nrm(k[15], (DEPTH, H_A, HS), 0.1),
        'rw_gn_g': 1.0 + nrm(k[16], (DEPTH, D_A), 0.05),
        'rw_gn_b': nrm(k[17], (DEPTH, D_A), 0.01),
        'rw_v0': nrm(k[18], (DEPTH - 1, D_A), 0.1),
        'rw_v1': nrm(k[19], (DEPTH - 1, D_A, R_V), D_A ** -0.5),
        'rw_v2': nrm(k[20], (DEPTH - 1, R_V, D_A), R_V ** -0.5),
        'cmp_w1': nrm(k[21], (DEPTH, 2, CMP_LEN * HD, CMP_HID), (CMP_LEN * HD) ** -0.5),
        'cmp_b1': nrm(k[22], (DEPTH, 2, CMP_HID), 0.01),
        'cmp_w2': nrm(k[23], (DEPTH, 2, CMP_HID, HD), CMP_HID ** -0.5),
        'cmp_b2': nrm(k[24], (DEPTH, 2, HD), 0.01),
        'rel_bias': nrm(k[25], (NUM_BUCKETS, H_B), 0.5),
        'w_up_a': nrm(k[26], (DEPTH, D_A, D_MODEL), BETA * D_A ** -0.5),
        'w_up_b': nrm(k[27], (DEPTH, D_B, D_MODEL), BETA * D_B ** -0.5),
        'w_out': nrm(k[28], (DEPTH, D_MODEL, D_MODEL), BETA * D_MODEL ** -0.5),
        'ln_g': 1.0 + nrm(k[29], (DEPTH, D_MODEL), 0.05),
        'ln_b': nrm(k[30], (DEPTH, D_MODEL), 0.01),
    }

def reference(x_prompt, x_sample, cache_kv, cache_win_kv, state_wkv, state_shift, page_table,
              w_in, mu_shift, rw_w0, rw_w2, rw_a0, rw_a2, rw_kk, rw_ka, rw_rk, rw_gn_g, rw_gn_b,
              rw_v0, rw_v1, rw_v2, cmp_w1, cmp_b1, cmp_w2, cmp_b2, rel_bias,
              w_up_a, w_up_b, w_out, ln_g, ln_b):
    p = {'w_in': w_in, 'mu_shift': mu_shift, 'rw_w0': rw_w0, 'rw_w2': rw_w2, 'rw_a0': rw_a0,
         'rw_a2': rw_a2, 'rw_kk': rw_kk, 'rw_ka': rw_ka, 'rw_rk': rw_rk, 'rw_gn_g': rw_gn_g,
         'rw_gn_b': rw_gn_b, 'rw_v0': rw_v0, 'rw_v1': rw_v1, 'rw_v2': rw_v2, 'cmp_w1': cmp_w1,
         'cmp_b1': cmp_b1, 'cmp_w2': cmp_w2, 'cmp_b2': cmp_b2, 'rel_bias': rel_bias,
         'w_up_a': w_up_a, 'w_up_b': w_up_b, 'w_out': w_out, 'ln_g': ln_g, 'ln_b': ln_b}
    dec_b, n_pages = page_table.shape
    y_p, y_s = x_prompt, x_sample
    vf_p, vf_s = None, None
    st_p, st_s = [], []
    for l in range(DEPTH):
        y_p, vf_p, sp = trunk_layer(y_p, l, vf_p, None, p)
        past = {'kv': cache_kv[l][page_table].reshape(dec_b, n_pages * PAGE_SIZE, 4, G_KV, HD),
                'win': cache_win_kv[l], 'wkv': state_wkv[l], 'shift': state_shift[l]}
        y_s, vf_s, ss = trunk_layer(y_s, l, vf_s, past, p)
        st_p.append(sp)
        st_s.append(ss)
    kv_rows_prompt = jnp.stack([s[0] for s in st_p])
    win_kv_prompt = jnp.stack([s[1] for s in st_p])
    wkv_prompt = jnp.stack([s[2] for s in st_p])
    shift_prompt = jnp.stack([s[3] for s in st_p])
    kv_rows_sample = jnp.stack([s[0] for s in st_s])
    win_kv_sample = jnp.stack([s[1] for s in st_s])
    wkv_sample = jnp.stack([s[2] for s in st_s])
    shift_sample = jnp.stack([s[3] for s in st_s])
    return (y_p, y_s, kv_rows_prompt, win_kv_prompt, wkv_prompt, shift_prompt,
            kv_rows_sample, win_kv_sample, wkv_sample, shift_sample)


_drawn_inputs = setup_inputs


def setup_inputs(seed=0):
    import zlib

    import numpy as np

    out = dict(_drawn_inputs(seed))
    spreads = {}
    factors = {'cache_kv': 5.859,
     'rw_kk': 15.877,
     'rw_rk': 4.161,
     'rw_gn_g': 8.0,
     'rw_gn_b': 64.0,
     'cmp_w1': 4.407,
     'cmp_b1': 34.983,
     'cmp_w2': 3.22,
     'cmp_b2': 64.0,
     'rel_bias': 8.0,
     'ln_b': 3.852}
    for name, (base, spread) in spreads.items():
        noise = np.random.default_rng([zlib.crc32(name.encode()), seed]).standard_normal(out[name].shape)
        drawn = base * np.exp(spread * noise) if base else spread * noise
        out[name] = __import__('jax').numpy.asarray(drawn.astype(out[name].dtype))
    for name, factor in factors.items():
        out[name] = (out[name] * factor).astype(out[name].dtype)
    return out
```

```python
import math
from contextlib import ExitStack

import numpy as np
import concourse.bass as bass
from concourse import mybir

F32 = mybir.dt.float32
I32 = mybir.dt.int32
ALU = mybir.AluOpType
ACT = mybir.ActivationFunctionType
AX = mybir.AxisListType

P = 128
D = 2048
KT = D // P
SEQ, NB = 256, 8
T = SEQ + NB
W1 = T + 1
DEPTH = 2
HD = 64
PAGE = 128
NG, NH = 4, 16
DA = 1024
A_TILES = 33
R0, K0, V0, LO, Z0 = 0, 8, 16, 24, 25
Q0, KV0, GL, ZB0 = 33, 41, 53, 54
H_TILES = 62
C = 64
NCH = SEQ // C
NPAIR = 8
LEVELS = 5
NBLK = 15
NSQ = NB + 1
KEYS = SEQ + 1
A_COLS = 4224
IN_COLS = 11952
GL_COL = 6784
TAIL_COL = GL_COL + 48
NEG = -1e30
ALPHA = (2 * DEPTH) ** 0.25
LN_EPS, GN_EPS = 1e-5, 64e-5
DECAY = -math.exp(-0.5)
SCALE = HD ** -0.5
TILE_PAIRS = 63
MU, PW0, PA0, PKK, PKA, PRK, PGG, PGB, PV0 = 0, 33, 41, 49, 57, 65, 73, 81, 89
N_ROWS = 97
LNG, LNB, CB1 = 97, 113, 129
N_PAR = 131
W0H, A0H, V0H, KA1 = 131, 139, 147, 155


def bucket(d):
    if d < 16:
        return max(d, 0)
    return min(31, 16 + int(math.log(d / 16) / math.log(8) * 16 + 1e-9))


def constants():
    p = np.arange(P)
    same = (p[:, None] // C) == (p[None, :] // C)
    strict = same & (p[:, None] < p[None, :])
    incl = same & (p[:, None] <= p[None, :])
    lv = []
    for m in (1, 2, 4, 8, 16, 32):
        lv.append((p[:, None] // (2 * m) == p[None, :] // (2 * m)) & (p[:, None] % (2 * m) < m) & (p[None, :] % (2 * m) >= m))
    mats = [np.eye(P), np.full((P, P), 1.0), same, strict, incl] + lv + [lv[0].T]
    scan = np.tile((np.arange(SEQ) % C != 0)[None], (P, 1))
    c = np.concatenate([np.asarray(m, np.float32) for m in mats] + [scan.astype(np.float32)], 1)
    rows = np.zeros((P, 2), np.float32)
    rows[:, 0] = p >= 31
    rows[:, 1] = 1.0
    c = np.concatenate([c, rows], 1)
    hot = np.zeros((33, 512 + KEYS + NBLK), np.float32)
    for u in range(512):
        if u <= 255:
            hot[bucket(255 - u), u] = 1
        else:
            hot[32, u] = NEG
    for k in range(KEYS):
        hot[bucket(SEQ - k), 512 + k] = 1
    for n in range(NBLK):
        hot[bucket(SEQ - 16 * n - 31), 512 + KEYS + n] = 1
    pick = np.zeros((48, 3, 16), np.float32)
    for h in range(16):
        for b in range(3):
            pick[3 * h + b, b, h] = 1
    return c, hot, pick.reshape(48, 48)


ARENA_N = 12020
N_PAR_DMA = 17
N_CONST = 12 * P + SEQ + 2
IDENT, ONES, BLOCK, STRICT, INCL, LV0 = 0, 1, 2, 3, 4, 5


class Steps:

    def __init__(self, sem, names):
        self.sem, self.names, self.k = sem, names.split(), 0
        self.n = len(self.names)

    def at(self, it, name):
        return it * self.n + (self.names.index(name) + 2)

    def past(self, it):
        return it * self.n + 1

    def done(self, ins, name):
        assert self.names[self.k % self.n] == name, (name, self.names[self.k % self.n])
        self.k += 1
        ins.then_inc(self.sem, 1)


def hybrid_trunk(nc, ins, outs):
    (x_prompt, x_sample, cache_kv, cache_win, state_wkv, state_shift, page_table, w_in, mu_shift,
     rw_w0, rw_w2, rw_a0, rw_a2, rw_kk, rw_ka, rw_rk, rw_gg, rw_gb, rw_v0, rw_v1, rw_v2,
     cmp_w1, cmp_b1, cmp_w2, cmp_b2, rel_bias, w_up_a, w_up_b, w_out, ln_g, ln_b,
     c_mats, c_hot, c_pick) = ins
    (y_prompt, y_sample, kv_prompt, win_prompt, wkv_prompt, shift_prompt,
     kv_sample, win_sample, wkv_sample, shift_sample) = outs
    bias_rows = nc.dram_tensor("bias_rows", (NH, P, 3 * P), F32).ap()
    new_rows = nc.dram_tensor("new_rows", (NB, 12 * P), F32).ap()
    n_phys = cache_kv.shape[1]

    with ExitStack() as ctx:
        def sb(name, shape, dt=F32):
            return ctx.enter_context(nc.sbuf_tensor(name, shape, dt))

        def sem(name):
            return ctx.enter_context(nc.semaphore(name))

        XT = sb("XT", [P, KT, T])
        H = sb("H", [P, H_TILES, W1])
        WT = sb("WT", [P, 2, KT, P])
        CM = sb("CM", [P, N_CONST])
        TAB = sb("TAB", [33, NH])
        PICK = sb("PICK", [48, 48])
        TOEP = sb("TOEP", [P, NH, 2 * P])
        BS = sb("BS", [NH, KEYS + NBLK])
        PT = sb("PT", [P, 163])
        SHT = sb("SHT", [P, NB * A_TILES])
        VF = sb("VF", [P, 8, T])
        FIRST = sb("FIRST", [P, 1])
        KVT = sb("KVT", [P, 3, 12 * P])
        GT = sb("GT", [P, 2, 48])
        GS = sb("GS", [NH, 3, NB])
        KCT = sb("KCT", [P, 2, NSQ * NBLK])
        KNVC = sb("KNVC", [P, NSQ * 4 * HD])
        KN = KNVC[:, 0:8 * T].rearrange("p (t n) -> p t n", n=T)
        VC = KNVC[0:NBLK, :].rearrange("p (s n) -> p s n", n=4 * HD)
        V1 = sb("V1", [P, 8, 32])
        B2K = sb("B2K", [P, 1])
        B2V = sb("B2V", [NBLK, HD])
        PAGES = sb("PAGES", [1, 2 * NB], I32)
        ARENA = sb("ARENA", [P, ARENA_N])
        used = [0]

        def fresh():
            used[0] = 0

        def take(rows, *shape):
            n = int(np.prod(shape))
            a = ARENA[0:rows, used[0]:used[0] + n]
            used[0] += n
            assert used[0] <= ARENA_N, used
            if len(shape) == 2:
                a = a.rearrange("p (a b) -> p a b", b=shape[1])
            if len(shape) == 3:
                a = a.rearrange("p (a b c) -> p a b c", b=shape[1], c=shape[2])
            return a

        PB = ctx.enter_context(nc.psum_tensor("PB", [P, 8, 512], F32))

        def cm(i, n=1):
            return CM[:, i * P:(i + n) * P]

        SCAN = CM[:, 12 * P:12 * P + SEQ]
        ROWOK = CM[:, 12 * P + SEQ:12 * P + SEQ + 1]
        ident = cm(IDENT)

        fresh()
        PRW, LNW, SSH = take(N_ROWS, P), take(34, P), take(88, 3, P)
        XTOK = take(P, 3, D)
        HOT, G16 = take(33, 512 + KEYS + NBLK), take(NH, 512)
        fresh()
        DIF, SHO, SHS = take(P, 11, T), take(P, 9, A_TILES), take(99, 3, P)
        SG = take(48, T)
        fresh()
        TLO, VV1, SQ = take(P, T), take(32, T), take(P, 8, T)
        used[0] -= 8 * T
        WA2, V2W, TH = take(P, P), take(32, P), take(P, 3, T)
        LW, AV, CS = take(P, T), take(P, 2, T), take(P, SEQ)
        GP, GI = take(P, NCH, C + 1), take(P, SEQ)
        TMP, BB, KP, RK, VS = (take(P, T) for _ in range(5))
        KF = RK
        AR = take(P, NCH, 2, C)
        BT, KTT, BC, KC = (take(P, SEQ) for _ in range(4))
        LT, RB, AK, RKK, YY = (take(P, 4, P) for _ in range(5))
        LM = take(P, 4, P)
        XX = take(P, 8, P)
        TOK = take(P, 3, 2, P)
        RS, US = take(P, 2, C), take(P, 2, C)
        ST = take(P, 2, P)
        WKO = take(P, C)
        SV = take(P, 6, C)
        used[0] = 0
        S4, M4 = take(P, C, C), take(P, C, C)
        VEC, SA, YS, YS2 = take(P, 6, C), take(P, C), take(P, C), take(C, P)
        fresh()
        SQG, TZ = take(P, 8, T), take(P, 8, T)
        fresh()
        CTX = take(P, 2, NSQ, SEQ)
        W1D = take(P, 32, P)
        PGS, W2, HX, HY, HT = take(P, 2, SEQ), take(P, HD), take(P, 4, 135), take(P, 4, 135), take(P, 4, 135)
        fresh()
        QS, KD, KCD, VG, VCG = take(P, 2, T), take(P, 2, SEQ), take(P, 16), take(P, 4, HD), take(NBLK, HD)
        SS, SC, NM, RSM, RR, CG = take(P, 2, 3 * P), take(P, 2, 16), take(P, 2, 3), take(P, 2, 3), take(P, 2, 3), take(P, 2, 3)
        PTS, PCT = take(P, 2, 3 * P), take(NBLK, SEQ)
        SPG, SWN, NEWR = take(P, 2, 512), take(P, 2, 512), take(1, 12 * P)
        KTS, QALL, QBD = take(P, 2, 2, KEYS), take(P, 32, NB), take(P, 2, NH)
        SAS, SCS, VCB, KCB = take(NH, 2, KEYS), take(NH, 16), take(NBLK, 256), take(P, 2, NBLK)
        NMS, RSS, RRS, CGS = take(NH, 3), take(NH, 3), take(NH, 3), take(NH, 3)
        PTT, PNT, PCC, OALL = take(P, 64), take(1, 32), take(NBLK, NH), take(P, 32, NB)
        fresh()
        LSQ, LST = take(P, KT, T), take(P, T)
        fresh()
        YO = take(P, 3, D)

        d_const, d_bias, d_toep, d_par, d_lora, d_w1, d_page = (sem(n) for n in (
            "const_loaded", "bias_stored", "bias_loaded", "params_loaded", "lora_loaded", "cmp_loaded", "page_loaded"))
        d_new, d_newin, d_state, d_att = (sem(n) for n in ("new_rows_stored", "x_loaded", "states_loaded", "att_loaded"))
        st_shift, st_kv, st_wkv, st_swkv, st_y = (sem(n) for n in (
            "shift_stored", "kv_stored", "wkv_stored", "sample_wkv_stored", "y_stored"))
        w_in_slot = [sem("weights_in_slot0"), sem("weights_in_slot1")]
        tile_done = [sem("tile_done0"), sem("tile_done1")]
        tile_out = [sem("tile_out0"), sem("tile_out1")]
        kv_turned, kv_out, x_turned, x_in, y_turned, y_out = (sem(n) for n in (
            "kv_turned", "kv_taken", "x_turned", "x_taken", "y_turned", "y_taken"))
        rows_free, wko_free = sem("rows_stored"), sem("pair_state_stored")
        passed = sem("passed")
        S = {}

        def steps(phase, **engines):
            for e, names in engines.items():
                S[phase + "_" + e] = Steps(sem(phase + "_" + e), names)

        steps("set", t="bias x", v="one bias x")
        lv = range(1, LEVELS + 1)
        ch = range(NCH)
        steps("par", t="rows shift", v="rows shift half half2 ka")
        steps("mix", v="sho " + " ".join(f"p{r} s{r} m{r}" for r in range(3)) + " gate", t="shift kv gates pick",
              a="tanh shift " + "kv gates pick")
        steps("low", v="kk sq max rs kn", a="lo vv sqrt", t="vv ss")
        steps("rw",
              t="low bon a1 tok x2 " + " ".join(f"y{j} z{j}" for j in lv) + " " + " ".join(f"r{c} u{c} o{c} s{c}" for c in ch) + " fin",
              a="th exp sv tok x2 " + " ".join(f"y{j}" for j in lv) + " " + " ".join(f"r{c} u{c} o{c}" for c in ch) + " fin",
              v="lw one gate cum vf1 vf2 vd vg vm kb kf kp rk at rt bt kt bc kc bon lt rb ak rkk x0 x1 lm1 "
                + " ".join(f"lm{j + 1} z{j}" for j in range(1, LEVELS)) + f" z{LEVELS} st "
                + " ".join(f"s{c}" for c in ch))
        steps("rs", t="vec y", v="vec m1 sa w m2 s1 m3 s2 m4 y y2 out")
        steps("gn", t="mu var", v="yc eps rs yn aff bon sz out", a="sq sqrt tanh")
        steps("cp", t="tr", a="ctx")
        steps("cm", t="h out", v="seq x x2 x3 x4 g out", a="th")
        steps("ap", a=" ".join(f"stg{e} " + " ".join(f"exp{e}{j} pt{e}{j}" for j in range(4)) for e in range(2)),
              t=" ".join(f"sc{e}{j} pt{e}{j} o{e}{j}" for e in range(2) for j in range(4)),
              v=" ".join((f"qs{e} " if j == 0 else "") + f"add{e}{j} max{e}{j} rc{e}{j} cg{e}{j} ok{e}{j} ps{e}{j} pt{e}{j}" + (f" o{e}{j}" if j % 2 else "")
                         for e in range(2) for j in range(4)))
        steps("aq", v="zero q back")
        steps("as", t="kt sc pt o", a="kt exp pt", v="kq add max rc cg ps o")
        steps("zb", a="tanh", v="sz out")
        steps("up", v="a b")
        steps("xa", a="scale")
        steps("ln", t="mu var", v="yc eps rs yn aff flag", a="sq sqrt")
        steps("fin", t="tr", a="tr")

        def on(eng, key, it, name):
            eng.wait_ge(S[key].sem, S[key].at(it, name))

        def before(eng, key, it):
            eng.wait_ge(S[key].sem, S[key].past(it))

        def alone(eng):
            eng.sem_inc(passed, 1)

        def mark(key, ins, name):
            S[key].done(ins, name)

        tiles = TILE_PAIRS
        J_G, J_UP, J_OUT = 31, 47, 55

        block = ctx.enter_context(nc.Block())

        @block.sync
        def _(sp):
            def load(s, src, at):
                n = src.shape[1]
                sp.dma_start(WT[:, s, at:at + 8, 0:n], src.rearrange("(k p) n -> p k n", p=P)).then_inc(w_in_slot[s], 16)

            def pair(L, j, srcs):
                for s, src in enumerate(srcs):
                    sp.wait_ge(tile_done[s], 1 + L * tiles + j)
                    first, second = src if isinstance(src, tuple) else (src[0:D // 2], src[D // 2:D])
                    load(s, first, 0)
                    load(s, second, 8)

            with sp.Fori(0, DEPTH) as L:
                def cols(w, c):
                    return w[L, :, bass.ds(c, P)]

                with sp.Fori(0, 26) as i:
                    pair(L, i, [cols(w_in, i * 256), cols(w_in, i * 256 + 128)])
                pair(L, 26, [cols(w_in, 52 * P), w_in[L, :, GL_COL:GL_COL + 48]])
                with sp.Fori(0, 20) as i:
                    pair(L, i + 27, [cols(w_in, i * 256 + TAIL_COL), cols(w_in, i * 256 + TAIL_COL + 128)])
                with sp.Fori(0, 8) as i:
                    pair(L, i + J_UP, [(cols(w_up_a, i * 256 + 128 * s), cols(w_up_b, i * 256 + 128 * s)) for s in range(2)])
                with sp.Fori(0, 8) as i:
                    pair(L, i + J_OUT, [cols(w_out, i * 256 + 128 * s) for s in range(2)])

        @block.gpsimd
        def _(po):
            def after(key, it, name=None):
                if name:
                    on(po, key, it, name)
                else:
                    before(po, key, it)
                alone(po)

            def stored(s, value):
                po.wait_ge(s, value)
                alone(po)

            def dma(out, in_, s):
                po.dma_start(out, in_).then_inc(s, 16)

            for counter in [x.sem for x in S.values()] + tile_done + tile_out + [rows_free, wko_free]:
                po.sem_inc(counter, 1)
            dma(CM[:, :], c_mats, d_const)
            dma(HOT[:, :], c_hot, d_const)
            dma(PICK[:, :], c_pick, d_const)
            dma(TAB[0:32, :], rel_bias, d_const)
            dma(PAGES[0:1, :], page_table.rearrange("(a b) n -> a (b n)", a=1), d_newin)
            dma(XTOK[:, 0:2, :], x_prompt[0].rearrange("(t p) d -> p t d", p=P), d_newin)
            dma(XTOK[0:NB, 2, :], x_sample.rearrange("b s d -> (b s) d"), d_newin)
            on(po, "set_v", 0, "bias")
            dma(bias_rows, G16[:, 0:3 * P].unsqueeze(1).broadcast_to([NH, P, 3 * P]), d_bias)
            po.wait_ge(d_bias, 16)
            dma(TOEP[:, :, :], bass.AP(bias_rows.tensor, P - 1, [[3 * P - 1, P], [3 * P * P, NH], [1, 2 * P]]), d_toep)
            po.wait_ge(d_newin, 48)

            with po.Fori(0, DEPTH) as L:
                after("ln_v", L)
                after("set_v", 0, "x")
                r = 0
                for w, n in ((mu_shift, 33), (rw_w0, 8), (rw_a0, 8), (rw_kk, 8), (rw_ka, 8)):
                    dma(PRW[r:r + n, :], w[L].rearrange("(t p) -> t p", p=P), d_par)
                    r += n
                dma(PRW[r:r + 8, :], rw_rk[L].rearrange("(t a) j -> t (a j)", a=2), d_par)
                for w, n in ((rw_gg, 8), (rw_gb, 8)):
                    r += 8
                    dma(PRW[r:r + n, :], w[L].rearrange("(t p) -> t p", p=P), d_par)
                dma(PRW[PV0:PV0 + 8, :], rw_v0[0].rearrange("(t p) -> t p", p=P), d_par)
                dma(LNW[0:16, :], ln_g[L].rearrange("(t p) -> t p", p=P), d_par)
                dma(LNW[16:32, :], ln_b[L].rearrange("(t p) -> t p", p=P), d_par)
                dma(LNW[32:34, :], cmp_b1[L], d_par)
                dma(SSH[:, :, :], state_shift[L].rearrange("b c -> (b c)").rearrange("(q p c) -> p q c", p=88, c=P), d_par)
                dma(V1[:, :, :], rw_v1[0].rearrange("(t p) n -> p t n", p=P), d_par)
                for a in range(2):
                    dma(B2K[a * HD:a * HD + HD, :], cmp_b2[L, 0].rearrange("(d o) -> d o", o=1), d_par)
                dma(B2V[:, :], cmp_b2[L, 1].partition_broadcast(NBLK), d_par)

                after("mix_a", L, "shift")
                dma(shift_prompt[L, 0].rearrange("(t p) -> t p", p=P), SHS[0:33, 0, :], st_shift)
                ss = shift_sample[L].rearrange("b c -> (b c)").rearrange("(r c) -> r c", c=P)
                dma(ss[0:66], SHS[33:99, 0, :], st_shift)
                dma(ss[66:165], SHS[:, 1, :], st_shift)
                dma(ss[165:264], SHS[:, 2, :], st_shift)
                after("mix_a", L, "kv")
                dma(new_rows, KVT[0:NB, 2, :], d_new)
                dma(kv_prompt[L, 0].rearrange("(t p) a g d -> p t (a g d)", p=P), KVT[:, 0:2, 0:8 * P], st_kv)
                dma(win_prompt[L, 0].rearrange("(t p) a g d -> p t (a g d)", p=P), KVT[:, 0:2, 8 * P:12 * P], st_kv)
                dma(kv_sample[L].rearrange("b s a g d -> b (s a g d)"), KVT[0:NB, 2, 0:8 * P], st_kv)
                dma(win_sample[L, :, SEQ - 1].rearrange("b a g d -> b (a g d)"), KVT[0:NB, 2, 8 * P:12 * P], st_kv)
                dma(win_sample[L, :, 0:SEQ - 1].rearrange("b w a g d -> b (w a g d)"),
                    cache_win[L, :, 1:SEQ].rearrange("b w a g d -> b (w a g d)"), st_kv)
                stored(st_shift, (L + 1) * 64)

                with po.Fori(0, NPAIR) as hp:
                    it = L * NPAIR + hp
                    after("mix_v", L, "gate")
                    after("low_v", L, "kn")
                    after("mix_t", L, "pick")
                    after("rw_t", it)
                    dma(WA2[0:C, :], rw_w2[L, :, bass.ds(hp * P, P)], d_lora)
                    dma(WA2[C:P, :], rw_a2[L, :, bass.ds(hp * P, P)], d_lora)
                    dma(V2W[:, :], rw_v2[0, :, bass.ds(hp * P, P)], d_lora)
                    after("rw_a", it, "fin")
                    dma(wkv_prompt[L, 0, bass.ds(hp * 2, 2)].rearrange("a i j -> (a i) j"), WKO[:, :], st_wkv)
                    stored(st_wkv, (it + 1) * 16)
                    po.sem_inc(wko_free, 1)
                after("rw_v", (L + 1) * NPAIR)
                for h2 in range(2):
                    for hp in range(NPAIR):
                        dma(S4[h2 * C + hp * 8:h2 * C + hp * 8 + 8, :, :], state_wkv[L, :, hp * 2 + h2], d_state)
                after("rs_v", L, "s2")
                for h2 in range(2):
                    for hp in range(NPAIR):
                        dma(wkv_sample[L, :, hp * 2 + h2], S4[h2 * C + hp * 8:h2 * C + hp * 8 + 8, :, :], st_swkv)
                stored(st_swkv, (L + 1) * 256)
                after("gn_v", L, "out")
                after("gn_a", L, "tanh")

                for kd in range(2):
                    after("cm_t", L * 2 + kd)
                    for a in range(2):
                        dma(W1D[a * HD:a * HD + HD, :, :], cmp_w1[L, kd].rearrange("(s d) n -> d s n", d=HD), d_w1)
                    dma(W2[:, :], cmp_w2[L, kd], d_w1)
                    with po.Fori(0, NB) as b:
                        it = (L * 2 + kd) * NB + b
                        after("cp_t", it)
                        for pg in range(2):
                            page = po.value_load(PAGES[0:1, bass.ds(b * 2 + pg, 1)], min_val=0, max_val=n_phys - 1)
                            dma(PGS[:, pg, :], cache_kv[L, page, :, kd].rearrange("p g d -> p (g d)"), d_page)
                after("cm_v", L * 2 + 1, "out")
                stored(d_new, (L + 1) * 16)
                stored(st_kv, (L + 1) * 80)
                po.sem_inc(rows_free, 1)
                with po.Fori(0, NB) as b:
                    it = L * NB + b
                    after("as_t", it)
                    for pg in range(2):
                        page = po.value_load(PAGES[0:1, bass.ds(b * 2 + pg, 1)], min_val=0, max_val=n_phys - 1)
                        dma(SPG[:, pg, :], cache_kv[L, page, :, 2:4].rearrange("p a g d -> p (a g d)"), d_att)
                    dma(SWN[:, :, :], cache_win[L, b].rearrange("(t p) a g d -> p t (a g d)", p=P), d_att)
                    dma(NEWR[0:1, :], new_rows[bass.ds(b, 1), :], d_att)
            after("fin_a", 0, "tr")
            dma(y_prompt[0].rearrange("(t p) d -> p t d", p=P), YO[:, 0:2, :], st_y)
            dma(y_sample.rearrange("b s d -> (b s) d"), YO[0:NB, 2, :], st_y)
            po.wait_ge(st_y, 32)
            po.wait_ge(st_shift, DEPTH * 64)
            po.wait_ge(st_kv, DEPTH * 80)
            po.wait_ge(st_wkv, DEPTH * NPAIR * 16)
            po.wait_ge(st_swkv, DEPTH * 256)

        @block.tensor
        def _(pe):
            mm, tr = nc.tensor.matmul, nc.tensor.transpose

            def transpose(out, in_):
                return tr(out, in_, ident[0:in_.shape[0], 0:in_.shape[0]])

            def project(L, j, s, bank, m=P, rhs=None, split=False):
                pe.wait_ge(w_in_slot[s], (L * tiles + j + 1) * 32)
                pe.wait_ge(tile_out[s], 1 + L * tiles + j)
                for k in range(KT):
                    if split:
                        o, st, sp_ = PB[0:m, (2 if k < 8 else 4) + s, 0:T], k % 8 == 0, k % 8 == 7
                    else:
                        o, st, sp_ = PB[0:m, bank, 0:T], k == 0, k == KT - 1
                    last = mm(o, WT[:, s, k, 0:m], rhs(k), start=st, stop=sp_)
                last.then_inc(tile_done[s], 1)

            def xs(k):
                return XT[:, k, :]

            pe.wait_ge(d_const, 64)
            on(pe, "set_v", 0, "one")
            mm(PB[0:NH, 0, :], TAB[:, :], HOT[:, 0:512], start=True, stop=True)
            mark("set_t", mm(PB[0:NH, 1, 0:KEYS + NBLK], TAB[:, :], HOT[:, 512:], start=True, stop=True), "bias")
            pe.wait_ge(d_newin, 48)
            for r in range(2):
                if r:
                    pe.wait_ge(x_in, 1)
                else:
                    on(pe, "set_v", 0, "bias")
                for q in range(8):
                    k = r * 8 + q
                    for t in range(2):
                        transpose(PB[:, q, t * P:t * P + P], XTOK[:, t, k * P:k * P + P])
                    last = transpose(PB[:, q, SEQ:T], XTOK[0:NB, 2, k * P:k * P + P])
                if r:
                    mark("set_t", last, "x")
                else:
                    last.then_inc(x_turned, 1)

            with pe.Fori(0, DEPTH) as L:
                pe.wait_ge(d_par, (L + 1) * (16 * N_PAR_DMA))
                on(pe, "set_v", 0, "x")
                transpose(PB[:, 0, 0:N_ROWS], PRW[:, :])
                mark("par_t", transpose(PB[:, 0, N_ROWS:N_PAR], LNW[:, :]), "rows")
                for q in range(3):
                    last = transpose(PB[:, 1, q * 88:q * 88 + 88], SSH[:, q, :])
                mark("par_t", last, "shift")

                on(pe, "par_v", L, "shift")
                alone(pe)
                with pe.Fori(0, 26) as i:
                    for s in range(2):
                        project(L, i, s, s, rhs=xs)
                project(L, 26, 0, 0, rhs=xs)
                project(L, 26, 1, 1, m=48, rhs=xs)
                with pe.Fori(0, 4) as i:
                    for s in range(2):
                        project(L, i + 27, s, s, rhs=xs)

                on(pe, "mix_v", L, "sho")
                sho = SHO.rearrange("p b t -> p (b t)")
                for q in range(3):
                    last = transpose(PB[0:99, 2, q * P:q * P + P], sho[:, q * 99:q * 99 + 99])
                mark("mix_t", last, "shift")
                for n in range(12):
                    if n >= 2:
                        pe.wait_ge(kv_out, L * 11 + (n - 1))
                    for t in range(2):
                        transpose(PB[:, 3 + n % 2, t * P:t * P + P], H[:, KV0 + n, 1 + t * P:1 + t * P + P])
                    last = transpose(PB[0:NB, 3 + n % 2, SEQ:SEQ + P], H[:, KV0 + n, 1 + SEQ:1 + T])
                    if n < 11:
                        last.then_inc(kv_turned, 1)
                mark("mix_t", last, "kv")
                on(pe, "mix_v", L, "gate")
                alone(pe)
                for t in range(2):
                    last = transpose(PB[:, 6, t * 48:t * 48 + 48], SG[:, t * P:t * P + P])
                mark("mix_t", last, "gates")
                for b in range(3):
                    last = mm(PB[0:NH, 7, b * NB:b * NB + NB], PICK[:, b * NH:b * NH + NH], SG[:, SEQ:T], start=True, stop=True)
                mark("mix_t", last, "pick")

                on(pe, "mix_v", L, "m2")
                for k in range(8):
                    last = mm(PB[0:32, 0, 0:T], V1[:, k, :], H[:, V0 + k, 1:W1], start=k == 0, stop=k == 7)
                mark("low_t", last, "vv")
                on(pe, "low_v", L, "sq")
                on(pe, "low_a", L, "vv")
                on(pe, "mix_a", L, "pick")
                for k in range(8):
                    last = mm(PB[:, k, 0:T], cm(BLOCK), SQ[:, k, :], start=True, stop=True)
                mark("low_t", last, "ss")

                with pe.Fori(0, NPAIR) as hp:
                    it = L * NPAIR + hp

                    def wait(*pairs):
                        for key, name in pairs:
                            on(pe, key, it, name)

                    pe.wait_ge(d_lora, (it + 1) * 48)
                    on(pe, "low_v", L, "kn")
                    on(pe, "low_a", L, "vv")
                    before(pe, "rw_a", it)
                    before(pe, "rw_v", it)
                    mm(PB[:, 0, 0:T], WA2[0:C, :], TLO[0:C, :], start=True, stop=True)
                    mm(PB[:, 1, 0:T], WA2[C:P, :], TLO[C:P, :], start=True, stop=True)
                    mark("rw_t", mm(PB[:, 2, 0:T], V2W[:, :], VV1[:, :], start=True, stop=True), "low")
                    wait(("rw_v", "rk"), ("rw_a", "th"))
                    mark("rw_t", mm(PB[:, 0, 0:T], cm(BLOCK), RK[:, :], start=True, stop=True), "bon")
                    wait(("rw_v", "kt"), ("rw_v", "rt"))
                    for src, bank in ((BT, 3), (KTT, 5)):
                        for q in range(4):
                            a, p = q // 2, q % 2
                            ra = slice(a * C, a * C + C)
                            last = mm(PB[:, bank + a, p * 256:p * 256 + 256], src[ra, p * P:p * P + P],
                                      AR[ra, 2 * p:2 * p + 2].rearrange("p c a n -> p (c a n)"), start=True, stop=True)
                    mark("rw_t", last, "a1")
                    wait(("rw_v", "kc"),)
                    for i, src in enumerate((VS, BC, KC)):
                        for p in range(2):
                            last = transpose(PB[:, 1 + i // 2, (i % 2) * 256 + p * P:(i % 2) * 256 + p * P + P],
                                             src[:, p * P:p * P + P])
                    mark("rw_t", last, "tok")
                    wait(("rw_v", "x1"),)
                    for q in range(4):
                        last = transpose(PB[:, 7, q * P:q * P + P], XX[:, 2 * q + 1, :])
                    mark("rw_t", last, "x2")
                    for j in lv:
                        wait(("rw_v", f"lm{j}"), ("rw_v", "rkk" if j == 1 else f"z{j - 1}"), *((("rw_a", "x2"),) if j == 1 else ()))
                        for q in range(4):
                            last = mm(PB[:, 3, q * P:q * P + P], LM[:, q, :], XX[:, 2 * q, :], start=True, stop=True)
                        mark("rw_t", last, f"y{j}")
                        wait(("rw_a", f"y{j}"),)
                        for q in range(4):
                            if j < LEVELS:
                                mm(PB[:, 5 + q // 2, (q % 2) * 256:(q % 2) * 256 + P], XX[:, 2 * q + 1, :], YY[:, q, :],
                                   start=True, stop=True)
                            last = mm(PB[:, 5 + q // 2, (q % 2) * 256 + P:(q % 2) * 256 + 2 * P], YY[:, q, :], XX[:, 2 * q + 1, :],
                                      start=True, stop=True)
                        mark("rw_t", last, f"z{j}")
                    wait(("rw_a", "tok"), ("rw_v", f"z{LEVELS}"), ("rw_v", "st"))
                    for c in ch:
                        p, b = c // 2, C * (c % 2)
                        rb = slice(b, b + C)
                        if c:
                            wait(("rw_v", f"s{c - 1}"),)
                        mm(PB[rb, 4, 0:P], AR[:, c, 0, :], ST[:, c % 2, :], start=True, stop=True)
                        for a in range(2):
                            q = 2 * a + p
                            last = mm(PB[rb, 4, a * C:a * C + C], AK[rb, q, b:b + C], TOK[rb, 0, p, a * C:a * C + C],
                                      start=False, stop=True, skip_group_check=True)
                        mark("rw_t", last, f"r{c}")
                        wait(("rw_a", f"r{c}"),)
                        alone(pe)
                        for a in range(2):
                            last = mm(PB[rb, 6, a * C:a * C + C], XX[rb, 2 * (2 * a + p) + 1, b:b + C], RS[rb, a, :],
                                      start=True, stop=True)
                        mark("rw_t", last, f"u{c}")
                        wait(("rw_a", f"u{c}"), *((("rw_a", f"o{c - 1}"),) if c else ()))
                        mm(PB[:, 7, 0:C], ST[:, c % 2, :], AR[:, c, 1, :], start=True, stop=True)
                        for a in range(2):
                            ra, q = slice(a * C, a * C + C), 2 * a + p
                            mm(PB[ra, 7, 0:C], US[rb, a, :], RB[rb, q, b:b + C], start=False, stop=False, skip_group_check=True)
                            last = mm(PB[ra, 7, 0:C], TOK[rb, 0, p, a * C:a * C + C], RKK[rb, q, b:b + C], start=False, stop=True,
                                      skip_group_check=True)
                        mark("rw_t", last, f"o{c}")
                        for a in range(2):
                            ra = slice(a * C, a * C + C)
                            mm(PB[ra, 3, 0:C], TOK[rb, 1, p, a * C:a * C + C], US[rb, a, :], start=True, stop=False)
                            last = mm(PB[ra, 3, 0:C], TOK[rb, 2, p, a * C:a * C + C], TOK[rb, 0, p, a * C:a * C + C],
                                      start=False, stop=True)
                        mark("rw_t", last, f"s{c}")
                    wait(("rw_v", f"s{NCH - 1}"),)
                    mark("rw_t", transpose(PB[:, 4, 0:P], ST[:, NCH % 2, :]), "fin")

                before(pe, "rw_a", (L + 1) * NPAIR)
                alone(pe)
                for q in range(6):
                    last = transpose(PB[0:C, q // 4, (q % 4) * P:(q % 4) * P + P], SV[:, q, :])
                mark("rs_t", last, "vec")
                on(pe, "rs_v", L, "y2")
                alone(pe)
                mark("rs_t", transpose(PB[:, 2, 0:C], YS2[:, :]), "y")

                on(pe, "rs_v", L, "out")
                for k in range(8):
                    last = mm(PB[:, k, 0:T], cm(BLOCK), H[:, R0 + k, 1:W1], start=True, stop=True)
                mark("gn_t", last, "mu")
                on(pe, "gn_a", L, "sq")
                for k in range(8):
                    last = mm(PB[:, k, 0:T], cm(BLOCK), SQG[:, k, :], start=True, stop=True)
                mark("gn_t", last, "var")

                on(pe, "gn_v", L, "eps")
                alone(pe)
                for kd in range(2):
                    ik = L * 2 + kd
                    with pe.Fori(0, NB) as b:
                        it = ik * NB + b
                        pe.wait_ge(d_page, (it + 1) * 32)
                        before(pe, "cp_a", it)
                        for t in range(2):
                            for pg in range(2):
                                last = transpose(PB[:, 0, t * 256 + pg * P:t * 256 + pg * P + P], PGS[:, pg, t * P:t * P + P])
                        mark("cp_t", last, "tr")
                    before(pe, "cp_a", (ik + 1) * NB)
                    on(pe, "cm_v", ik, "seq")
                    pe.wait_ge(d_w1, (ik + 1) * 48)
                    for g in range(NG):
                        rg = slice((g % 2) * HD, (g % 2) * HD + HD)
                        for s in range(32):
                            last = mm(PB[:, 2 + g, 0:NSQ * NBLK], W1D[rg, s, :],
                                      CTX[rg, g // 2, :, s:s + 16 * (NBLK - 1) + 1:16], start=s == 0, stop=s == 31)
                    mark("cm_t", last, "h")
                    on(pe, "cm_v", ik, "g")
                    if kd == 0:
                        for g in range(NG):
                            last = mm(PB[(g % 2) * HD:(g % 2) * HD + HD, 6, (g // 2) * 135:(g // 2) * 135 + 135],
                                      W2[:, :], HX[:, g, :], start=True, stop=True)
                    else:
                        for s in range(NSQ):
                            for g in range(NG):
                                last = mm(PB[0:NBLK, 2 + s // 2, (s % 2) * 256 + g * HD:(s % 2) * 256 + g * HD + HD],
                                          HX[:, g, s * NBLK:s * NBLK + NBLK], W2[:, :], start=True, stop=True)
                    mark("cm_t", last, "out")

                with pe.Fori(0, 2) as g2:
                    it = L * 2 + g2
                    on(pe, "cm_v", L * 2 + 1, "out")
                    for e in range(2):
                        for j in range(4):
                            rj = slice((j % 2) * HD, (j % 2) * HD + HD)
                            if j == 0:
                                on(pe, "ap_v", it, f"qs{e}")
                                on(pe, "ap_a", it, f"stg{e}")
                            if e + j:
                                on(pe, "ap_v", it, f"add{e if j else 0}{j - 1 if j else 3}")
                            else:
                                before(pe, "ap_v", it)
                            for br in range(2):
                                mm(PB[:, br, 0:P], QS[rj, j // 2, 0:P], KD[rj, br, 0:P], start=True, stop=True)
                                mm(PB[:, br, P:3 * P], QS[rj, j // 2, P:2 * P], KD[rj, br, :], start=True, stop=True)
                            for t in range(2):
                                last = mm(PB[:, 2, t * 16:t * 16 + NBLK], QS[rj, j // 2, t * P:t * P + P], KCD[rj, 0:NBLK],
                                          start=True, stop=True)
                            mark("ap_t", last, f"sc{e}{j}")
                            on(pe, "ap_v", it, f"ps{e}{j}")
                            for br in range(2):
                                transpose(PB[:, 3 + br, 0:P], SS[:, br, 0:P])
                                transpose(PB[:, 3 + br, P:2 * P], SS[:, br, P:2 * P])
                                transpose(PB[:, 3 + br, 2 * P:3 * P], SS[:, br, 2 * P:3 * P])
                            for t in range(2):
                                last = transpose(PB[0:NBLK, 5, t * P:t * P + P], SC[:, t, 0:NBLK])
                            mark("ap_t", last, f"pt{e}{j}")
                            on(pe, "ap_a", it, f"pt{e}{j}")
                            on(pe, "ap_v", it, f"pt{e}{j}")
                            o = PB[rj, 6, 0:SEQ]
                            if j % 2 == 0 and e + j:
                                on(pe, "ap_v", it, f"o{e if j else 0}{j - 1 if j else 3}")
                            for br in range(2):
                                mm(o, VG[:, 2 * br, :], PTS[:, br, 0:SEQ], start=br == 0, stop=False)
                                mm(PB[rj, 6, P:SEQ], VG[:, 2 * br + 1, :], PTS[:, br, SEQ:3 * P], start=False, stop=False)
                            mark("ap_t", mm(o, VCG[:, :], PCT[:, :], start=False, stop=True), f"o{e}{j}")

                with pe.Fori(0, NB) as b:
                    it = L * NB + b
                    on(pe, "aq_v", L, "q")
                    pe.wait_ge(d_att, (it + 1) * 64)
                    before(pe, "as_a", it)
                    before(pe, "as_v", it)
                    for br, src in enumerate((SPG, SWN)):
                        for t in range(2):
                            for pg in range(2):
                                last = transpose(PB[:, br, t * 256 + pg * P:t * 256 + pg * P + P], src[:, pg, t * P:t * P + P])
                    mark("as_t", last, "kt")
                    on(pe, "as_a", it, "kt")
                    on(pe, "as_v", it, "kq")
                    for br in range(2):
                        for t in range(2):
                            mm(PB[0:NH, 2 + br, 0:KEYS], QBD[:, t, :], KTS[:, br, t, :], start=t == 0, stop=t == 1)
                    for t in range(2):
                        last = mm(PB[0:NH, 4, 0:NBLK], QBD[:, t, :], KCB[:, t, :], start=t == 0, stop=t == 1)
                    mark("as_t", last, "sc")
                    on(pe, "as_v", it, "ps")
                    alone(pe)
                    for br in range(2):
                        for pg in range(2):
                            transpose(PB[:, 5, (br * 2 + pg) * NH:(br * 2 + pg) * NH + NH], SAS[:, br, pg * P:pg * P + P])
                        transpose(PB[0:1, 5, 64 + br * NH:64 + br * NH + NH], SAS[:, br, SEQ:KEYS])
                    mark("as_t", transpose(PB[0:NBLK, 5, 96:96 + NH], SCS[:, 0:NBLK]), "pt")
                    on(pe, "as_a", it, "pt")
                    for t in range(2):
                        o = PB[:, 6, t * NH:t * NH + NH]
                        for pg in range(2):
                            mm(o, SPG[:, pg, 256 + t * P:256 + t * P + P], PTT[:, pg * NH:pg * NH + NH], start=pg == 0, stop=False)
                            mm(o, SWN[:, pg, 256 + t * P:256 + t * P + P], PTT[:, (2 + pg) * NH:(2 + pg) * NH + NH],
                               start=False, stop=False)
                        for br, c0 in enumerate((6 * P, 10 * P)):
                            mm(o, NEWR[0:1, c0 + t * P:c0 + t * P + P], PNT[0:1, br * NH:br * NH + NH], start=False, stop=False)
                        last = mm(o, VCB[:, t * P:t * P + P], PCC[:, :], start=False, stop=True)
                    mark("as_t", last, "o")

                on(pe, "zb_v", L, "out")
                on(pe, "gn_v", L, "out")
                alone(pe)
                with pe.Fori(0, 16) as i:
                    for s in range(2):
                        project(L, i + J_G, s, s, rhs=xs)
                with pe.Fori(0, 8) as i:
                    for s in range(2):
                        project(L, i + J_UP, s, None, rhs=lambda k: H[:, (Z0 if k < 8 else ZB0 - 8) + k, 1:W1], split=True)
                pe.wait_ge(tile_out[1], 1 + L * tiles + J_OUT)
                pe.wait_ge(tile_out[0], 1 + L * tiles + J_OUT)
                alone(pe)
                with pe.Fori(0, 8) as i:
                    for s in range(2):
                        project(L, i + J_OUT, s, s, rhs=lambda k: H[:, k, 1:W1])

                pe.wait_ge(tile_out[1], 1 + (L + 1) * tiles)
                pe.wait_ge(tile_out[0], 1 + (L + 1) * tiles)
                for k in range(KT):
                    last = mm(PB[:, 0, 0:T], cm(ONES), XT[:, k, :], start=k == 0, stop=k == KT - 1)
                mark("ln_t", last, "mu")
                on(pe, "ln_a", L, "sq")
                for k in range(KT):
                    last = mm(PB[:, 1, 0:T], cm(ONES), LSQ[:, k, :], start=k == 0, stop=k == KT - 1)
                mark("ln_t", last, "var")

            before(pe, "ln_v", DEPTH)
            for q in range(12):
                if q >= 8:
                    pe.wait_ge(y_out, q - 7)
                t, k4 = q // 4, q % 4
                for k in range(4):
                    if t < 2:
                        last = transpose(PB[:, q % 8, k * P:k * P + P], XT[:, 4 * k4 + k, t * P:t * P + P])
                    else:
                        last = transpose(PB[0:NB, q % 8, k * P:k * P + P], XT[:, 4 * k4 + k, SEQ:T])
                if q < 11:
                    last.then_inc(y_turned, 1)
            mark("fin_t", last, "tr")

        @block.scalar
        def _(sc):
            act = nc.scalar.activation

            def copy(out, in_):
                return act(out, in_, ACT.Copy)

            def take_out(L, j, s, out, func=ACT.Copy, m=P, scale=1.0):
                sc.wait_ge(tile_done[s], 1 + L * tiles + j + 1)
                act(out, PB[0:m, s, 0:T], func, scale=scale).then_inc(tile_out[s], 1)

            sc.wait_ge(d_const, 64)
            with sc.Fori(0, DEPTH) as L:
                with sc.Fori(0, 26) as i:
                    for s in range(2):
                        take_out(L, i, s, H[:, i * 2 + s, 1:W1])
                take_out(L, 26, 0, H[:, 52, 1:W1])
                take_out(L, 26, 1, H[0:48, GL, 1:W1], m=48)
                with sc.Fori(0, 4) as i:
                    for s in range(2):
                        take_out(L, i + 27, s, H[:, i * 2 + (ZB0 + s), 1:W1])

                sc.wait_ge(tile_out[1], 1 + L * tiles + 31)
                on(sc, "par_v", L, "shift")
                mark("mix_a", act(SG[:, :], H[0:48, GL, 1:W1], ACT.Tanh, scale=0.5), "tanh")
                on(sc, "mix_t", L, "shift")
                mark("mix_a", copy(SHS.rearrange("p a b -> p (a b)"), PB[0:99, 2, 0:3 * P]), "shift")
                for n in range(12):
                    if n < 11:
                        sc.wait_ge(kv_turned, L * 11 + (n + 1))
                    else:
                        on(sc, "mix_t", L, "kv")
                    if n == 0:
                        sc.wait_ge(rows_free, L + 1)
                    copy(KVT[:, 0:2, n * P:n * P + P], PB[:, 3 + n % 2, 0:SEQ].rearrange("p (t n) -> p t n", n=P))
                    last = copy(KVT[0:NB, 2, n * P:n * P + P], PB[0:NB, 3 + n % 2, SEQ:SEQ + P])
                    if n < 11:
                        last.then_inc(kv_out, 1)
                mark("mix_a", last, "kv")
                on(sc, "mix_t", L, "gates")
                mark("mix_a", copy(GT.rearrange("p a b -> p (a b)"), PB[:, 6, 0:96]), "gates")
                on(sc, "mix_t", L, "pick")
                mark("mix_a", copy(GS.rearrange("p a b -> p (a b)"), PB[0:NH, 7, 0:24]), "pick")

                on(sc, "mix_v", L, "m2")
                act(TLO[0:C, :], H[0:C, LO, 1:W1], ACT.Tanh)
                mark("low_a", copy(TLO[C:P, :], H[C:P, LO, 1:W1]), "lo")
                on(sc, "low_t", L, "vv")
                mark("low_a", copy(VV1[:, :], PB[0:32, 0, 0:T]), "vv")
                on(sc, "low_v", L, "max")
                mark("low_a", act(SQ[:, :, :], SQ[:, :, :], ACT.Sqrt), "sqrt")

                with sc.Fori(0, NPAIR) as hp:
                    it = L * NPAIR + hp

                    def wait(*pairs):
                        for key, name in pairs:
                            on(sc, key, it, name)

                    before(sc, "rw_v", it)
                    on(sc, "low_v", L, "kn")
                    wait(("rw_t", "low"),)
                    for i, col in enumerate((W0H, A0H, V0H)):
                        last = act(TH[:, i, :], PB[:, i, 0:T], ACT.Tanh, bias=PT[:, bass.ds(hp + col, 1)], scale=0.5)
                    mark("rw_a", last, "th")
                    wait(("rw_v", "cum"), ("rw_v", "one"))
                    act(GP[:, :, 1:C + 1], CS.rearrange("p (c n) -> p c n", n=C), ACT.Exp)
                    act(GI[:, :], CS[:, :], ACT.Exp, scale=-1.0)
                    last = act(SV[:, 1, bass.ds(hp * 8, 8)], LW[:, SEQ:T], ACT.Exp)
                    mark("rw_a", last, "exp")
                    wait(("rw_v", "kb"), ("rw_v", "kp"))
                    copy(SV[:, 0, bass.ds(hp * 8, 8)], H[:, hp, 1 + SEQ:W1])
                    copy(SV[:, 2, bass.ds(hp * 8, 8)], KP[:, SEQ:T])
                    copy(SV[:, 3, bass.ds(hp * 8, 8)], VS[:, SEQ:T])
                    copy(SV[:, 4, bass.ds(hp * 8, 8)], KN[:, hp, SEQ:T])
                    mark("rw_a", copy(SV[:, 5, bass.ds(hp * 8, 8)], BB[:, SEQ:T]), "sv")
                    wait(("rw_t", "tok"),)
                    copy(TOK[:, 0:2].rearrange("p a b n -> p (a b n)"), PB[:, 1, :])
                    mark("rw_a", copy(TOK[:, 2].rearrange("p b n -> p (b n)"), PB[:, 2, 0:SEQ]), "tok")
                    wait(("rw_t", "x2"),)
                    mark("rw_a", copy(XX[:, 0:8:2, :], PB[:, 7, :].rearrange("p (q n) -> p q n", n=P)), "x2")
                    for j in lv:
                        wait(("rw_t", f"y{j}"),)
                        mark("rw_a", copy(YY.rearrange("p q n -> p (q n)"), PB[:, 3, :]), f"y{j}")
                    for c in ch:
                        rb = slice(C * (c % 2), C * (c % 2) + C)
                        wait(("rw_t", f"r{c}"),)
                        mark("rw_a", copy(RS[rb].rearrange("p a n -> p (a n)"), PB[rb, 4, 0:P]), f"r{c}")
                        wait(("rw_t", f"u{c}"),)
                        mark("rw_a", copy(US[rb].rearrange("p a n -> p (a n)"), PB[rb, 6, 0:P]), f"u{c}")
                        wait(("rw_t", f"o{c}"), ("rw_v", "rt"))
                        mark("rw_a", copy(H[:, hp, 1 + c * C:1 + c * C + C], PB[:, 7, 0:C]), f"o{c}")
                    wait(("rw_t", "fin"),)
                    sc.wait_ge(wko_free, it + 1)
                    copy(WKO[0:C, :], PB[0:C, 4, 0:C])
                    mark("rw_a", copy(WKO[C:P, :], PB[C:P, 4, C:P]), "fin")

                sc.wait_ge(st_swkv, (L + 1) * 256)
                on(sc, "gn_v", L, "yc")
                mark("gn_a", act(SQG[:, :, :], H[:, 0:8, 1:W1], ACT.Square), "sq")
                on(sc, "gn_v", L, "eps")
                mark("gn_a", act(SQG[:, :, :], SQG[:, :, :], ACT.Sqrt), "sqrt")
                mark("gn_a", act(TZ[:, :, :], H[:, Z0:Z0 + 8, 1:W1], ACT.Tanh, scale=0.5), "tanh")

                for kd in range(2):
                    ik = L * 2 + kd
                    with sc.Fori(0, NB) as b:
                        it = ik * NB + b
                        on(sc, "cp_t", it, "tr")
                        on(sc, "gn_v", L, "out")
                        before(sc, "cm_t", ik)
                        mark("cp_a", copy(CTX[:, :, b, :], PB[:, 0, :].rearrange("p (t n) -> p t n", n=SEQ)), "ctx")
                    on(sc, "cm_v", ik, "x4")
                    mark("cm_a", act(HT[:, :, :], HY[:, :, :], ACT.Tanh, scale=0.7978845608028654), "th")

                with sc.Fori(0, 2) as g2:
                    it = L * 2 + g2
                    for e in range(2):
                        re = slice(e * HD, e * HD + HD)
                        if e == 0:
                            on(sc, "cm_v", L * 2 + 1, "out")
                            on(sc, "cm_t", L * 2 + 1, "out")
                            before(sc, "ap_t", it)
                        else:
                            on(sc, "ap_t", it, "o03")
                        for a in range(2):
                            ra = slice(a * HD, a * HD + HD)
                            for br in range(2):
                                copy(KD[ra, br, :], H[re, g2 + (KV0 + 4 + 4 * br), 1:1 + SEQ])
                            copy(KCD[ra, 0:NBLK], KCT[re, g2, 8 * NBLK:9 * NBLK])
                        for br in range(2):
                            for t in range(2):
                                copy(VG[:, 2 * br + t, :], KVT[:, t, bass.ds(g2 * P + ((6 + 4 * br) * P + e * HD), HD)])
                        mark("ap_a", copy(VCG[:, :], VC[:, 8, bass.ds(g2 * P + e * HD, HD)]), f"stg{e}")
                        for j in range(4):
                            on(sc, "ap_v", it, f"max{e}{j}")
                            for t in range(2):
                                w = slice(0, P) if t == 0 else slice(P, 3 * P)
                                act(SC[:, t, 0:NBLK], SC[:, t, 0:NBLK], ACT.Exp, bias=NM[:, t, 0:1], accum_out=RSM[:, t, 0:1])
                                for br in range(2):
                                    last = act(SS[:, br, w], SS[:, br, w], ACT.Exp, bias=NM[:, t, br + 1:br + 2],
                                               accum_out=RSM[:, t, br + 1:br + 2])
                            mark("ap_a", last, f"exp{e}{j}")
                            on(sc, "ap_t", it, f"pt{e}{j}")
                            mark("ap_a", copy(PTS[:, :, :], PB[:, 3:5, 0:3 * P]), f"pt{e}{j}")

                with sc.Fori(0, NB) as b:
                    it = L * NB + b
                    on(sc, "as_t", it, "kt")
                    before(sc, "as_v", it)
                    for br in range(2):
                        last = copy(KTS[:, br, :, 0:SEQ], PB[:, br, :].rearrange("p (t n) -> p t n", n=SEQ))
                    mark("as_a", last, "kt")
                    on(sc, "as_v", it, "max")
                    act(SCS[:, 0:NBLK], SCS[:, 0:NBLK], ACT.Exp, bias=NMS[:, 0:1], accum_out=RSS[:, 0:1])
                    for br in range(2):
                        last = act(SAS[:, br, :], SAS[:, br, :], ACT.Exp, bias=NMS[:, br + 1:br + 2],
                                   accum_out=RSS[:, br + 1:br + 2])
                    mark("as_a", last, "exp")
                    on(sc, "as_t", it, "pt")
                    copy(PTT[:, :], PB[:, 5, 0:64])
                    copy(PNT[:, :], PB[0:1, 5, 64:96])
                    mark("as_a", copy(PCC[:, :], PB[0:NBLK, 5, 96:96 + NH]), "pt")

                on(sc, "as_v", (L + 1) * NB - 1, "o")
                on(sc, "gn_v", L, "out")
                mark("zb_a", act(TZ[:, :, :], H[:, ZB0:ZB0 + 8, 1:W1], ACT.Tanh, scale=0.5), "tanh")

                on(sc, "zb_v", L, "out")
                with sc.Fori(0, 12) as i:
                    for s in range(2):
                        take_out(L, i + J_G, s, H[:, i * 2 + s, 1:W1], ACT.Tanh, scale=0.5)
                with sc.Fori(0, 4) as i:
                    for s in range(2):
                        take_out(L, i + (J_G + 12), s, H[:, i * 2 + (Q0 + s), 1:W1], ACT.Tanh, scale=0.5)
                sc.wait_ge(tile_done[1], 1 + L * tiles + J_UP)
                sc.wait_ge(tile_done[0], 1 + L * tiles + J_UP)
                mark("xa_a", act(XT[:, :, :], XT[:, :, :], ACT.Copy, scale=ALPHA), "scale")
                on(sc, "ln_v", L, "yc")
                mark("ln_a", act(LSQ[:, :, :], XT[:, :, :], ACT.Square), "sq")
                on(sc, "ln_v", L, "eps")
                mark("ln_a", act(LST[:, :], LST[:, :], ACT.Sqrt), "sqrt")

            for q in range(12):
                if q < 11:
                    sc.wait_ge(y_turned, q + 1)
                else:
                    on(sc, "fin_t", 0, "tr")
                t, k4, m = q // 4, q % 4, (P if q < 8 else NB)
                last = copy(YO[0:m, t, k4 * 512:k4 * 512 + 512], PB[0:m, q % 8, :])
                if q < 11:
                    last.then_inc(y_out, 1)
            mark("fin_a", last, "tr")

        @block.vector
        def _(ve):
            tt, ts, stt = nc.vector.tensor_tensor, nc.vector.tensor_scalar, nc.vector.scalar_tensor_tensor
            cp, red, recip = nc.vector.tensor_copy, nc.vector.tensor_reduce, nc.vector.reciprocal

            def spread(a, *shape):
                return a.broadcast_to(list(shape))

            ve.wait_ge(d_const, 64)
            nc.vector.memset(H[:, :, 0:1], 0.0)
            nc.vector.memset(VF[:, :, :], 0.0)
            nc.vector.memset(FIRST[:, :], 1.0)
            mark("set_v", nc.vector.memset(TAB[32:33, :], 1.0), "one")
            on(ve, "set_t", 0, "bias")
            cp(G16[:, :], PB[0:NH, 0, :])
            mark("set_v", cp(BS[:, :], PB[0:NH, 1, 0:KEYS + NBLK]), "bias")
            ve.wait_ge(x_turned, 1)
            cp(XT[:, 0:8, :], PB[:, :, 0:T]).then_inc(x_in, 1)
            on(ve, "set_t", 0, "x")
            mark("set_v", cp(XT[:, 8:16, :], PB[:, :, 0:T]), "x")

            with ve.Fori(0, DEPTH) as L:
                def own(key, name):
                    on(ve, key, L, name)

                own("par_t", "rows")
                mark("par_v", cp(PT[:, 0:N_PAR], PB[:, 0, 0:N_PAR]), "rows")
                own("par_t", "shift")
                mark("par_v", cp(SHT[:, :], PB[:, 1, 0:NB * A_TILES]), "shift")
                own("par_v", "rows")
                mark("par_v", ts(PT[:, W0H:W0H + 16], PT[:, PW0:PW0 + 16], 0.5, None, ALU.mult), "half")
                mark("par_v", ts(PT[:, V0H:V0H + 8], PT[:, PV0:PV0 + 8], 0.5, None, ALU.mult), "half2")
                mark("par_v", ts(PT[:, KA1:KA1 + 8], PT[:, PKA:PKA + 8], -1.0, 1.0, ALU.mult, ALU.add), "ka")

                for s in range(2):
                    ve.wait_ge(tile_out[s], 1 + L * tiles + J_G)
                own("par_v", "ka")
                mark("mix_v", cp(SHO[:, :, :], H[:, 0:A_TILES, SEQ:W1].rearrange("p t b -> p b t")), "sho")
                sht = SHT.rearrange("p (b t) -> p t b", t=A_TILES)
                for r in range(3):
                    t0 = 11 * r
                    own("mix_v", f"m{r - 1}" if r else "sho")
                    mark("mix_v", tt(DIF[:, :, 0:SEQ], H[:, t0:t0 + 11, 0:SEQ], H[:, t0:t0 + 11, 1:1 + SEQ], ALU.subtract), f"p{r}")
                    mark("mix_v", tt(DIF[:, :, SEQ:T], sht[:, t0:t0 + 11, :], H[:, t0:t0 + 11, 1 + SEQ:W1], ALU.subtract), f"s{r}")
                    own("mix_v", f"s{r}")
                    for t in range(11):
                        last = stt(H[:, t0 + t, 1:W1], DIF[:, t, :], PT[:, MU + t0 + t:MU + t0 + t + 1], H[:, t0 + t, 1:W1],
                                   ALU.mult, ALU.add)
                    mark("mix_v", last, f"m{r}")
                own("mix_a", "tanh")
                mark("mix_v", ts(SG[:, :], SG[:, :], 0.5, 0.5, ALU.mult, ALU.add), "gate")

                own("mix_v", "m2")
                mark("low_v", tt(KN[:, :, :], H[:, K0:K0 + 8, 1:W1], spread(PT[:, PKK:PKK + 8].unsqueeze(2), P, 8, T), ALU.mult), "kk")
                own("low_v", "kk")
                mark("low_v", tt(SQ[:, :, :], KN[:, :, :], KN[:, :, :], ALU.mult), "sq")
                own("low_t", "ss")
                mark("low_v", ts(SQ[:, :, :], PB[:, :, 0:T], 1e-24, None, ALU.max), "max")
                own("low_a", "sqrt")
                mark("low_v", recip(SQ[:, :, :], SQ[:, :, :]), "rs")
                own("low_v", "rs")
                mark("low_v", tt(KN[:, :, :], KN[:, :, :], SQ[:, :, :], ALU.mult), "kn")

                with ve.Fori(0, NPAIR) as hp:
                    it = L * NPAIR + hp

                    def wait(*names):
                        for n in names:
                            key, name = n if isinstance(n, tuple) else ("rw_v", n)
                            on(ve, key, it, name)

                    def v(name, ins):
                        mark("rw_v", ins, name)

                    def par(col):
                        return PT[:, bass.ds(hp + col, 1)]

                    q4 = lambda a: a.rearrange("p (c n) -> p c n", n=C)
                    rr, kk, vv, vf = H[:, hp, 1:W1], H[:, hp + K0, 1:W1], H[:, hp + V0, 1:W1], VF[:, hp, :]
                    before(ve, "rw_a", it)
                    before(ve, "rw_v", it)
                    on(ve, "low_v", L, "kn")
                    wait(("rw_a", "th"))
                    v("lw", ts(LW[:, :], TH[:, 0, :], DECAY / 2, DECAY / 2, ALU.mult, ALU.add))
                    v("one", nc.vector.memset(GP[:, :, 0:1], 1.0))
                    v("gate", ts(AV[:, :, :], TH[:, 1:3, :], 0.5, 0.5, ALU.mult, ALU.add))
                    wait("lw")
                    v("cum", nc.vector.tensor_tensor_scan(CS[:, :], SCAN, LW[:, 0:SEQ], 0.0, ALU.mult, ALU.add))
                    v("vf1", tt(TMP[:, :], vv, vf, ALU.subtract))
                    wait("vf1")
                    v("vf2", stt(vf, TMP[:, :], FIRST[:, 0:1], vf, ALU.mult, ALU.add))
                    wait("vf2")
                    v("vd", tt(TMP[:, :], vf, vv, ALU.subtract))
                    wait("vd")
                    v("vg", tt(TMP[:, :], TMP[:, :], AV[:, 1, :], ALU.mult))
                    wait("vg")
                    v("vm", tt(VS[:, :], vv, TMP[:, :], ALU.add))
                    v("kb", tt(BB[:, :], KN[:, hp, :], AV[:, 0, :], ALU.mult))
                    v("kf", ts(KF[:, :], AV[:, 0, :], par(PKA), par(KA1), ALU.mult, ALU.add))
                    wait("kf")
                    v("kp", tt(KP[:, :], kk, KF[:, :], ALU.mult))
                    wait("kp")
                    v("rk", stt(RK[:, :], rr, par(PRK), KP[:, :], ALU.mult, ALU.mult))
                    wait(("rw_a", "exp"))
                    v("at", stt(AR[:, :, 0, :], q4(KN[:, hp, 0:SEQ]), -1.0, GP[:, :, 0:C], ALU.mult, ALU.mult))
                    v("rt", tt(AR[:, :, 1, :], q4(H[:, hp, 1:1 + SEQ]), GP[:, :, 1:C + 1], ALU.mult))
                    v("bt", tt(BT[:, :], BB[:, 0:SEQ], GI[:, :], ALU.mult))
                    v("kt", tt(KTT[:, :], KP[:, 0:SEQ], GI[:, :], ALU.mult))
                    wait("kt")
                    last_decay = spread(GP[:, :, C:C + 1], P, NCH, C)
                    v("bc", tt(q4(BC), q4(BT), last_decay, ALU.mult))
                    v("kc", tt(q4(KC), q4(KTT), last_decay, ALU.mult))
                    wait(("rw_t", "bon"))
                    v("bon", tt(H[:, hp + K0, 1:W1], PB[:, 0, 0:T], VS[:, :], ALU.mult))
                    p4 = lambda bank, x: PB[:, bank:bank + 2, :].rearrange("p h (c x n) -> p (h c) x n", x=2, n=C)[:, :, x, :]
                    m4 = lambda m: cm(m).rearrange("p (c n) -> p c n", n=C).unsqueeze(1)
                    o4 = lambda a: a.rearrange("p q (c n) -> p q c n", n=C)
                    wait(("rw_t", "a1"))

                    def masked(out, bank, x, m):
                        for q in range(2):
                            src = PB[:, bank + q, :].rearrange("p (a c x n) -> p x a c n", a=2, x=2, n=C)[:, x]
                            last = tt(o4(out[:, 2 * q:2 * q + 2]), src, spread(m4(m), P, 2, 2, C), ALU.mult)
                        return last

                    v("lt", masked(LT, 3, 0, STRICT))
                    v("rb", masked(RB, 3, 1, INCL))
                    v("ak", masked(AK, 5, 0, STRICT))
                    v("rkk", masked(RKK, 5, 1, INCL))
                    wait("lt")
                    xt = XX[:, 1:8:2, :]
                    v("x0", tt(xt, LT[:, :, :], spread(cm(LV0).unsqueeze(1), P, 4, P), ALU.mult))
                    wait("x0")
                    v("x1", tt(xt, xt, spread(ident.unsqueeze(1), P, 4, P), ALU.add))
                    v("lm1", tt(LM[:, :, :], LT[:, :, :], spread(cm(LV0 + 1).unsqueeze(1), P, 4, P), ALU.mult))
                    for j in range(1, LEVELS + 1):
                        wait(("rw_t", f"y{j}"))
                        if j < LEVELS:
                            v(f"lm{j + 1}", tt(LM[:, :, :], LT[:, :, :], spread(cm(LV0 + j + 1).unsqueeze(1), P, 4, P), ALU.mult))
                        wait(("rw_t", f"z{j}"))
                        z = PB[:, 5:7, :].rearrange("p h (q n) -> p (h q) n", n=P)
                        if j < LEVELS:
                            v(f"z{j}", tt(XX[:, :, :], XX[:, :, :], z, ALU.add))
                        else:
                            v(f"z{j}", tt(xt, xt, z[:, 1:8:2, :], ALU.add))
                    v("st", nc.vector.memset(ST[:, :, :], 0.0))
                    for c in ch:
                        wait(("rw_t", f"s{c}"), f"s{c - 1}" if c else "st")
                        for a in range(2):
                            ra = slice(a * C, a * C + C)
                            last = stt(ST[ra, (c + 1) % 2, ra], ST[ra, c % 2, ra], GP[ra, c, C:C + 1], PB[ra, 3, 0:C],
                                       ALU.mult, ALU.add)
                        v(f"s{c}", last)

                own("rs_t", "vec")
                for a in range(2):
                    cp(VEC[a * C:a * C + C, 0:4, :], PB[0:C, 0, :].rearrange("p (q n) -> p q n", n=P)[:, :, a * C:a * C + C])
                    last = cp(VEC[a * C:a * C + C, 4:6, :], PB[0:C, 1, 0:2 * P].rearrange("p (q n) -> p q n", n=P)[:, :, a * C:a * C + C])
                mark("rs_v", last, "vec")
                across = lambda q: spread(VEC[:, q:q + 1, :], P, C, C)
                down = lambda x: spread(x.unsqueeze(2), P, C, C)
                s4, m4_ = S4[:, :, :], M4[:, :, :]
                ve.wait_ge(d_state, (L + 1) * 256)
                own("rs_v", "vec")
                mark("rs_v", tt(m4_, s4, across(4), ALU.mult), "m1")
                own("rs_v", "m1")
                mark("rs_v", red(SA[:, :], m4_, AX.X, ALU.add), "sa")
                mark("rs_v", tt(s4, s4, across(1), ALU.mult), "w")
                own("rs_v", "w")
                mark("rs_v", tt(m4_, down(SA[:, :]), across(5), ALU.mult), "m2")
                own("rs_v", "m2")
                mark("rs_v", tt(s4, s4, m4_, ALU.subtract), "s1")
                own("rs_v", "s1")
                mark("rs_v", tt(m4_, down(VEC[:, 3, :]), across(2), ALU.mult), "m3")
                own("rs_v", "m3")
                mark("rs_v", tt(s4, s4, m4_, ALU.add), "s2")
                own("rs_v", "s2")
                mark("rs_v", tt(m4_, s4, across(0), ALU.mult), "m4")
                own("rs_v", "m4")
                mark("rs_v", red(YS[:, :], m4_, AX.X, ALU.add), "y")
                own("rs_v", "y")
                cp(YS2[:, 0:C], YS[0:C, :])
                mark("rs_v", cp(YS2[:, C:P], YS[C:P, :]), "y2")
                own("rs_t", "y")
                mark("rs_v", cp(H[:, R0:R0 + 8, 1 + SEQ:W1], PB[:, 2, 0:C].rearrange("p (h b) -> p h b", b=NB)), "out")

                y8 = H[:, R0:R0 + 8, 1:W1]
                own("gn_t", "mu")
                mark("gn_v", stt(y8, PB[:, :, 0:T], -1.0 / HD, y8, ALU.mult, ALU.add), "yc")
                own("gn_t", "var")
                mark("gn_v", ts(SQG[:, :, :], PB[:, :, 0:T], 1.0 / HD, GN_EPS, ALU.mult, ALU.add), "eps")
                own("gn_a", "sqrt")
                mark("gn_v", recip(SQG[:, :, :], SQG[:, :, :]), "rs")
                own("gn_v", "rs")
                mark("gn_v", tt(y8, y8, SQG[:, :, :], ALU.mult), "yn")
                own("gn_v", "yn")
                for t in range(8):
                    last = ts(H[:, R0 + t, 1:W1], H[:, R0 + t, 1:W1], PT[:, PGG + t:PGG + t + 1], PT[:, PGB + t:PGB + t + 1],
                              ALU.mult, ALU.add)
                mark("gn_v", last, "aff")
                own("gn_v", "aff")
                mark("gn_v", tt(y8, y8, H[:, K0:K0 + 8, 1:W1], ALU.add), "bon")
                own("gn_a", "tanh")
                mark("gn_v", stt(TZ[:, :, :], TZ[:, :, :], 1.0, H[:, Z0:Z0 + 8, 1:W1], ALU.add, ALU.mult), "sz")
                own("gn_v", "sz")
                mark("gn_v", stt(H[:, Z0:Z0 + 8, 1:W1], y8, 0.5, TZ[:, :, :], ALU.mult, ALU.mult), "out")

                own("gn_v", "out")
                for kd in range(2):
                    ik = L * 2 + kd

                    def wait2(*pairs):
                        for key, name in pairs:
                            on(ve, key, ik, name)

                    before(ve, "cm_t", ik)
                    mark("cm_v", cp(CTX[:, :, NB, :], H[:, KV0 + 2 * kd:KV0 + 2 * kd + 2, 1:1 + SEQ]), "seq")
                    wait2(("cm_t", "h"))
                    mark("cm_v", ts(HX[:, :, :], PB[:, 2:6, 0:135], PT[:, CB1 + kd:CB1 + kd + 1], None, ALU.add), "x")
                    wait2(("cm_v", "x"))
                    mark("cm_v", tt(HY[:, :, :], HX[:, :, :], HX[:, :, :], ALU.mult), "x2")
                    wait2(("cm_v", "x2"))
                    mark("cm_v", ts(HY[:, :, :], HY[:, :, :], 0.044715, 1.0, ALU.mult, ALU.add), "x3")
                    wait2(("cm_v", "x3"))
                    mark("cm_v", tt(HY[:, :, :], HY[:, :, :], HX[:, :, :], ALU.mult), "x4")
                    wait2(("cm_a", "th"))
                    mark("cm_v", stt(HX[:, :, :], HT[:, :, :], 1.0, HX[:, :, :], ALU.add, ALU.mult), "g")
                    wait2(("cm_t", "out"))
                    if kd == 0:
                        last = ts(KCT.rearrange("p a b -> p (a b)"), PB[:, 6, 0:270], 0.5, B2K[:, 0:1], ALU.mult, ALU.add)
                    else:
                        src = PB[0:NBLK, 2:7, :].rearrange("p a b -> p (a b)")[:, 0:NSQ * 256].rearrange("p (g d) -> p g d", d=HD)
                        last = stt(KNVC[0:NBLK, :].rearrange("p (g d) -> p g d", d=HD), src, 0.5,
                                   spread(B2V[:, :].unsqueeze(1), NBLK, NSQ * NG, HD), ALU.mult, ALU.add)
                    mark("cm_v", last, "out")

                ve.wait_ge(d_toep, 16)
                with ve.Fori(0, 2) as g2:
                    it = L * 2 + g2

                    def wait3(*pairs):
                        for key, name in pairs:
                            on(ve, key, it, name)

                    on(ve, "cm_v", L * 2 + 1, "out")
                    before(ve, "ap_t", it)
                    for e in range(2):
                        if e:
                            wait3(("ap_t", "o03"))
                        mark("ap_v", ts(QS[:, :, :], H[:, bass.ds(g2 * 4 + (Q0 + 2 * e), 2), 1:W1], SCALE, None, ALU.mult), f"qs{e}")
                        for j in range(4):
                            n = f"{e}{j}"
                            h = g2 * 8 + (4 * e + j)
                            wait3(("ap_t", "sc" + n))
                            nc.vector.memset(SC[:, 0, 7:16], NEG)
                            tt(SC[:, 0, 0:7], PB[:, 2, 0:7], TOEP[:, h, 159:256:16], ALU.add)
                            tt(SC[:, 1, 0:15], PB[:, 2, 16:31], TOEP[:, h, 31:256:16], ALU.add)
                            for br in range(2):
                                tt(SS[:, br, 0:P], PB[:, br, 0:P], TOEP[:, h, P:2 * P], ALU.add)
                                last = tt(SS[:, br, P:3 * P], PB[:, br, P:3 * P], TOEP[:, h, 0:2 * P], ALU.add)
                            mark("ap_v", last, "add" + n)
                            wait3(("ap_v", "add" + n))
                            red(NM[:, :, 0], SC[:, :, 0:NBLK], AX.X, ALU.max, negate=True)
                            red(NM[:, 0, 1:3], SS[:, :, 0:P], AX.X, ALU.max, negate=True)
                            mark("ap_v", red(NM[:, 1, 1:3], SS[:, :, P:3 * P], AX.X, ALU.max, negate=True), "max" + n)
                            wait3(("ap_a", "exp" + n))
                            mark("ap_v", recip(RR[:, :, :], RSM[:, :, :]), "rc" + n)
                            wait3(("ap_v", "rc" + n))
                            mark("ap_v", tt(CG[:, :, :], RR[:, :, :], GT[:, :, bass.ds(g2 * 24 + 3 * (4 * e + j), 3)], ALU.mult), "cg" + n)
                            wait3(("ap_v", "cg" + n))
                            mark("ap_v", ts(CG[:, 0, 0:1], CG[:, 0, 0:1], ROWOK, None, ALU.mult), "ok" + n)
                            wait3(("ap_v", "ok" + n))
                            for t in range(2):
                                w = slice(0, P) if t == 0 else slice(P, 3 * P)
                                ts(SC[:, t, 0:NBLK], SC[:, t, 0:NBLK], CG[:, t, 0:1], None, ALU.mult)
                                for br in range(2):
                                    last = ts(SS[:, br, w], SS[:, br, w], CG[:, t, br + 1:br + 2], None, ALU.mult)
                            mark("ap_v", last, "ps" + n)
                            wait3(("ap_t", "pt" + n))
                            mark("ap_v", cp(PCT[:, :], PB[0:NBLK, 5, 0:SEQ]), "pt" + n)
                            if j % 2:
                                wait3(("ap_t", "o" + n))
                                alone(ve)
                                mark("ap_v", cp(H[:, g2 * 4 + (Q0 + 2 * e + j // 2), 1:1 + SEQ], PB[:, 6, 0:SEQ]), "o" + n)

                on(ve, "cm_v", L * 2 + 1, "out")
                mark("aq_v", nc.vector.memset(QALL[:, :, :], 0.0), "zero")
                own("aq_v", "zero")
                hq = lambda g, a: H[a * HD:a * HD + HD, Q0 + 2 * g:Q0 + 2 * g + 2, 1 + SEQ:W1]
                part = lambda m, g, a: m[(g % 2) * HD:(g % 2) * HD + HD, (g // 2) * NH + 4 * g + a:(g // 2) * NH + 4 * g + 4:2, :]
                for g in range(NG):
                    for a in range(2):
                        last = ts(part(QALL, g, a), hq(g, a), SCALE, None, ALU.mult)
                mark("aq_v", last, "q")
                with ve.Fori(0, NB) as b:
                    it = L * NB + b

                    def wait4(*pairs):
                        for key, name in pairs:
                            on(ve, key, it, name)

                    on(ve, "aq_v", L, "q")
                    before(ve, "as_t", it)
                    before(ve, "as_a", it)
                    cp(QBD[:, :, :], QALL[:, :, bass.ds(b, 1)].rearrange("p (t h) o -> p t (h o)", t=2))
                    for br in range(2):
                        cp(KTS[:, br, :, SEQ:KEYS], H[:, KV0 + 4 + 4 * br:KV0 + 6 + 4 * br, bass.ds(b + (1 + SEQ), 1)])
                    cp(KCB[:, :, :], KCT[:, :, bass.ds(b * NBLK, NBLK)])
                    mark("as_v", cp(VCB[:, :], VC[:, b, :]), "kq")
                    wait4(("as_t", "sc"))
                    tt(SCS[:, 0:NBLK], PB[0:NH, 4, 0:NBLK], BS[:, KEYS:], ALU.add)
                    for br in range(2):
                        last = tt(SAS[:, br, :], PB[0:NH, 2 + br, 0:KEYS], BS[:, 0:KEYS], ALU.add)
                    mark("as_v", last, "add")
                    wait4(("as_v", "add"))
                    red(NMS[:, 0:1], SCS[:, 0:NBLK], AX.X, ALU.max, negate=True)
                    mark("as_v", red(NMS[:, 1:3], SAS[:, :, :], AX.X, ALU.max, negate=True), "max")
                    wait4(("as_a", "exp"))
                    mark("as_v", recip(RRS[:, :], RSS[:, :]), "rc")
                    wait4(("as_v", "rc"))
                    mark("as_v", tt(CGS[:, :], RRS[:, :], GS[:, :, bass.ds(b, 1)].rearrange("p a o -> p (a o)"), ALU.mult), "cg")
                    wait4(("as_v", "cg"))
                    ts(SCS[:, 0:NBLK], SCS[:, 0:NBLK], CGS[:, 0:1], None, ALU.mult)
                    for br in range(2):
                        last = ts(SAS[:, br, :], SAS[:, br, :], CGS[:, br + 1:br + 2], None, ALU.mult)
                    mark("as_v", last, "ps")
                    wait4(("as_t", "o"))
                    mark("as_v", cp(OALL[:, :, bass.ds(b, 1)], PB[:, 6, 0:32].unsqueeze(2)), "o")
                before(ve, "as_v", (L + 1) * NB)
                for g in range(NG):
                    for a in range(2):
                        last = cp(hq(g, a), part(OALL, g, a))
                mark("aq_v", last, "back")
                own("zb_a", "tanh")
                mark("zb_v", stt(TZ[:, :, :], TZ[:, :, :], 1.0, H[:, ZB0:ZB0 + 8, 1:W1], ALU.add, ALU.mult), "sz")
                own("aq_v", "back")
                own("zb_v", "sz")
                mark("zb_v", stt(H[:, ZB0:ZB0 + 8, 1:W1], H[:, Q0:Q0 + 8, 1:W1], 0.5, TZ[:, :, :], ALU.mult, ALU.mult), "out")

                for half, gb in ((0, V0), (8, Q0)):
                    with ve.Fori(0, 4) as i:
                        for s in range(2):
                            it = L * 16 + i * 2 + (half + s)
                            ga, gbt = H[:, i * 2 + (half + s), 1:W1], H[:, i * 2 + (gb + s), 1:W1]
                            ve.wait_ge(tile_done[s], 1 + L * tiles + i + (J_UP + half // 2 + 1))
                            ve.wait_ge(tile_out[s], 1 + L * tiles + J_UP)
                            mark("up_v", stt(ga, ga, 1.0, PB[:, 2 + s, 0:T], ALU.add, ALU.mult), "a")
                            mark("up_v", stt(gbt, gbt, 1.0, PB[:, 4 + s, 0:T], ALU.add, ALU.mult), "b")
                            on(ve, "up_v", it, "b")
                            tt(ga, ga, gbt, ALU.add).then_inc(tile_out[s], 1)
                with ve.Fori(0, 8) as i:
                    for s in range(2):
                        x = XT[:, i * 2 + s, :]
                        ve.wait_ge(tile_done[s], 1 + L * tiles + i + (J_OUT + 1))
                        on(ve, "xa_a", L, "scale")
                        stt(x, PB[:, s, 0:T], 0.5, x, ALU.mult, ALU.add).then_inc(tile_out[s], 1)
                own("ln_t", "mu")
                mark("ln_v", stt(XT[:, :, :], spread(PB[:, 0:1, 0:T], P, KT, T), -1.0 / D, XT[:, :, :], ALU.mult, ALU.add), "yc")
                own("ln_t", "var")
                mark("ln_v", ts(LST[:, :], PB[:, 1, 0:T], 1.0 / D, LN_EPS, ALU.mult, ALU.add), "eps")
                own("ln_a", "sqrt")
                mark("ln_v", recip(LST[:, :], LST[:, :]), "rs")
                own("ln_v", "rs")
                mark("ln_v", tt(XT[:, :, :], XT[:, :, :], spread(LST[:, :].unsqueeze(1), P, KT, T), ALU.mult), "yn")
                own("ln_v", "yn")
                for t in range(KT):
                    last = ts(XT[:, t, :], XT[:, t, :], PT[:, LNG + t:LNG + t + 1], PT[:, LNB + t:LNB + t + 1], ALU.mult, ALU.add)
                mark("ln_v", last, "aff")
                mark("ln_v", nc.vector.memset(FIRST[:, :], 0.0), "flag")


INPUTS = ["x_prompt", "x_sample", "cache_kv", "cache_win_kv", "state_wkv", "state_shift", "page_table", "w_in", "mu_shift",
          "rw_w0", "rw_w2", "rw_a0", "rw_a2", "rw_kk", "rw_ka", "rw_rk", "rw_gn_g", "rw_gn_b", "rw_v0", "rw_v1", "rw_v2",
          "cmp_w1", "cmp_b1", "cmp_w2", "cmp_b2", "rel_bias", "w_up_a", "w_up_b", "w_out", "ln_g", "ln_b"]
OUTPUTS = [(1, SEQ, D), (NB, 1, D), (DEPTH, 1, SEQ, 4, NG, HD), (DEPTH, 1, SEQ, 2, NG, HD), (DEPTH, 1, NH, HD, HD),
           (DEPTH, 1, A_COLS), (DEPTH, NB, 1, 4, NG, HD), (DEPTH, NB, SEQ, 2, NG, HD), (DEPTH, NB, NH, HD, HD),
           (DEPTH, NB, A_COLS)]


def kernel(**inputs):
    import numpy as _np
    import concourse.bacc as _bacc
    from concourse.bass_utils import run_bass_kernel_spmd as _run

    nc = _bacc.Bacc("TRN2", target_bir_lowering=False, num_devices=1)
    arrays, ins, outs = {}, [], []
    consts = dict(zip(("c_mats", "c_hot", "c_pick"), constants()))
    for name in INPUTS + list(consts):
        a = _np.ascontiguousarray(inputs[name] if name in inputs else consts[name])
        arrays[f"in_{name}"] = a
        ins.append(nc.dram_tensor(f"in_{name}", a.shape, mybir.dt.from_np(a.dtype), kind="ExternalInput").ap())
    for i, shape in enumerate(OUTPUTS):
        outs.append(nc.dram_tensor(f"out_{i}", shape, F32, kind="ExternalOutput").ap())
    hybrid_trunk(nc, ins, outs)
    r = _run(nc, [arrays], core_ids=[0])
    return tuple(r.results[0][f"out_{i}"] for i in range(len(OUTPUTS)))
```
